# Optimizing a Trainium2 kernel written in Bass

```python
import jax, jax.numpy as jnp
from jax import lax
import numpy as np

D_MODEL = 1024
BATCH = 1
SEQ = 256
DEPTH = 2

CHUNK = 64
N_A_LAYERS = DEPTH // 2
N_B_LAYERS = DEPTH - N_A_LAYERS
HEAD_DIM = 64
N_HEADS_A = D_MODEL // HEAD_DIM
N_HEADS_B = D_MODEL // HEAD_DIM
N_KV_HEADS_B = 4
GROUP_B = N_HEADS_B // N_KV_HEADS_B
WINDOW = 128
WINDOW_CHUNKS = WINDOW // CHUNK
Q_BLOCK = 128
D_FF = 2816
RMS_EPS = 1e-6
MACARON_WEIGHT = 0.5
N_NORMS = 6

kernel_name = "yoco_fox_swa_sink_macaron"

def rmsnorm(x, g):
    xf = x.astype(jnp.float32)
    y = xf * lax.rsqrt(jnp.mean(xf * xf, axis=-1, keepdims=True) + RMS_EPS)
    return (y * g.astype(jnp.float32)).astype(x.dtype)

def swiglu(h, w_gate, w_up, w_down):
    return (jax.nn.silu(h @ w_gate) * (h @ w_up)) @ w_down

def alibi_slopes(n):
    return 2.0 ** (-8.0 * jnp.arange(1, n + 1, dtype=jnp.float32) / n)

def fox_attention(q, k, v, log_f):
    b, s, h, d = q.shape
    nb = s // Q_BLOCK
    c = jnp.cumsum(log_f, axis=1).transpose(0, 2, 1)
    qb = q.reshape(b, nb, Q_BLOCK, h, d).transpose(1, 0, 2, 3, 4)
    cb = c.reshape(b, h, nb, Q_BLOCK).transpose(2, 0, 1, 3)
    kpos = jnp.arange(s)
    scale = HEAD_DIM ** -0.5

    def block(args):
        qi, ci, i = args
        logits = jnp.einsum('bqhd,bkhd->bhqk', qi, k).astype(jnp.float32) * scale
        logits = logits + ci[..., :, None] - c[:, :, None, :]
        qpos = i * Q_BLOCK + jnp.arange(Q_BLOCK)
        causal = kpos[None, :] <= qpos[:, None]
        logits = jnp.where(causal, logits, -jnp.inf)
        p = jax.nn.softmax(logits, axis=-1).astype(v.dtype)
        return jnp.einsum('bhqk,bkhd->bqhd', p, v)

    out = lax.map(block, (qb, cb, jnp.arange(nb)))
    return out.transpose(1, 0, 2, 3, 4).reshape(b, s, h * d)

def fox_mixer(h, w_in, b_f, w_o):
    b, s, _ = h.shape
    hd = N_HEADS_A * HEAD_DIM
    proj = h @ w_in
    q = proj[..., :hd].reshape(b, s, N_HEADS_A, HEAD_DIM)
    k = proj[..., hd:2 * hd].reshape(b, s, N_HEADS_A, HEAD_DIM)
    v = proj[..., 2 * hd:3 * hd].reshape(b, s, N_HEADS_A, HEAD_DIM)
    log_f = jax.nn.log_sigmoid(proj[..., 3 * hd:].astype(jnp.float32) + b_f.astype(jnp.float32))
    return fox_attention(q, k, v, log_f) @ w_o

def swa_sink_attention(q, k, v, sinks):
    b, s = q.shape[0], q.shape[1]
    nc = s // CHUNK
    w = WINDOW_CHUNKS

    def band(t):
        tc = t.reshape(b, nc, CHUNK, N_KV_HEADS_B, HEAD_DIM)
        tp = jnp.pad(tc, ((0, 0), (w - 1, 0), (0, 0), (0, 0), (0, 0)))
        return jnp.concatenate([tp[:, i:i + nc] for i in range(w)], axis=2)

    kb, vb = band(k), band(v)
    qc = q.reshape(b, nc, CHUNK, N_KV_HEADS_B, GROUP_B, HEAD_DIM)
    logits = jnp.einsum('bnqkgd,bnskd->bnkgqs', qc, kb).astype(jnp.float32) * (HEAD_DIM ** -0.5)
    qi = jnp.arange(CHUNK)
    kj = jnp.arange(w * CHUNK)
    dist = jnp.abs((w - 1) * CHUNK + qi[:, None] - kj[None, :]).astype(jnp.float32)
    slopes = alibi_slopes(N_HEADS_B).reshape(N_KV_HEADS_B, GROUP_B)
    logits = logits - slopes[:, :, None, None] * dist
    key_chunk = jnp.arange(nc)[:, None] - (w - 1) + kj[None, :] // CHUNK
    valid = key_chunk >= 0
    logits = jnp.where(valid[None, :, None, None, None, :], logits, -jnp.inf)
    sink = sinks.astype(jnp.float32).reshape(N_KV_HEADS_B, GROUP_B)[None, None, :, :, None]
    m = jnp.maximum(logits.max(axis=-1), sink)
    e = jnp.exp(logits - m[..., None])
    p = e / (e.sum(axis=-1) + jnp.exp(sink - m))[..., None]
    out = jnp.einsum('bnkgqs,bnskd->bnqkgd', p.astype(vb.dtype), vb)
    return out.reshape(b, s, N_HEADS_B * HEAD_DIM)

def setup_inputs(seed: int = 0) -> dict:
    key = jax.random.key(seed)
    ks = jax.random.split(key, 16)
    D, F = D_MODEL, D_FF
    hd_a = N_HEADS_A * HEAD_DIM
    hd_b = N_HEADS_B * HEAD_DIM
    kv_b = N_KV_HEADS_B * HEAD_DIM
    nrm = lambda k, shape, fan_in: jax.random.normal(k, shape, jnp.float32) * fan_in ** -0.5
    return {
        "x": jax.random.normal(ks[0], (BATCH, SEQ, D), jnp.float32),
        "ffn_w_gate": nrm(ks[1], (DEPTH, 2, D, F), D),
        "ffn_w_up": nrm(ks[2], (DEPTH, 2, D, F), D),
        "ffn_w_down": nrm(ks[3], (DEPTH, 2, F, D), F),
        "norm_g": 1.0 + 0.05 * jax.random.normal(ks[4], (DEPTH, N_NORMS, D), jnp.float32),
        "a_w_in": nrm(ks[5], (N_A_LAYERS, D, 3 * hd_a + N_HEADS_A), D),
        "a_b_f": jax.random.uniform(ks[6], (N_A_LAYERS, N_HEADS_A), jnp.float32, 1.0, 6.0),
        "a_w_o": nrm(ks[7], (N_A_LAYERS, hd_a, D), hd_a),
        "kv_norm_g": 1.0 + 0.05 * jax.random.normal(ks[8], (D,), jnp.float32),
        "b_w_kv": nrm(ks[9], (D, 2 * kv_b), D),
        "b_w_q": nrm(ks[10], (N_B_LAYERS, D, hd_b), D),
        "b_sinks": 0.5 * jax.random.normal(ks[11], (N_B_LAYERS, N_HEADS_B), jnp.float32),
        "b_w_o": nrm(ks[12], (N_B_LAYERS, hd_b, D), hd_b),
    }

def reference(x, ffn_w_gate, ffn_w_up, ffn_w_down, norm_g, a_w_in, a_b_f, a_w_o,
              kv_norm_g, b_w_kv, b_w_q, b_sinks, b_w_o):
    b, s, _ = x.shape
    kv_b = N_KV_HEADS_B * HEAD_DIM

    def macaron_half(x, l, j):
        h = rmsnorm(x, norm_g[l, 4 * j])
        y = swiglu(h, ffn_w_gate[l, j], ffn_w_up[l, j], ffn_w_down[l, j])
        return x + MACARON_WEIGHT * rmsnorm(y, norm_g[l, 4 * j + 1])

    k_shared = None
    v_shared = None
    for l in range(DEPTH):
        x = macaron_half(x, l, 0)
        h = rmsnorm(x, norm_g[l, 2])
        if l < N_A_LAYERS:
            y = fox_mixer(h, a_w_in[l], a_b_f[l], a_w_o[l])
        else:
            j = l - N_A_LAYERS
            q = (h @ b_w_q[j]).reshape(b, s, N_HEADS_B, HEAD_DIM)
            y = swa_sink_attention(q, k_shared, v_shared, b_sinks[j]) @ b_w_o[j]
        x = x + rmsnorm(y, norm_g[l, 3])
        x = macaron_half(x, l, 1)
        if l == N_A_LAYERS - 1:
            kv = rmsnorm(x, kv_norm_g) @ b_w_kv
            k_shared = kv[..., :kv_b].reshape(b, s, N_KV_HEADS_B, HEAD_DIM)
            v_shared = kv[..., kv_b:].reshape(b, s, N_KV_HEADS_B, HEAD_DIM)
    return x


_drawn_inputs = setup_inputs


def setup_inputs(seed=0):
    import zlib

    import numpy as np

    out = dict(_drawn_inputs(seed))
    spreads = {}
    factors = {}
    for name, (base, spread) in spreads.items():
        noise = np.random.default_rng([zlib.crc32(name.encode()), seed]).standard_normal(out[name].shape)
        drawn = base * np.exp(spread * noise) if base else spread * noise
        out[name] = __import__('jax').numpy.asarray(drawn.astype(out[name].dtype))
    for name, factor in factors.items():
        out[name] = (out[name] * factor).astype(out[name].dtype)
    return out
```

```python
from contextlib import ExitStack

import numpy as np

import concourse.bass as bass
from concourse import mybir

F32 = mybir.dt.float32
F32R = mybir.dt.float32r
ALU = mybir.AluOpType
ACT = mybir.ActivationFunctionType
AX = mybir.AxisListType

P = 128
NB = 2
D = 1024
DC = D // P
F = 2816
FC = 256
STEPS = F // FC
DH = 64
H = D // DH
PAIRS = H // 2
KVH = 4
COLS = 512
RING = 3
DMAS = 2
EPS = 1e-6
SEG = 3 * P
MASKED = -1.0e38
FAR = 1.0e38
GAINS = 3

GU = (0, 1)
HT = 2
Y = 4
SC = (0, 1)
PTB = (2, 3)
OT = 4
CB = 5


def constants():
    k, s = np.arange(P)[:, None], np.arange(P)[None, :]
    ident = np.eye(P)
    tri = k <= s
    diag = np.where(s <= k, 0.0, MASKED)
    causal = np.concatenate([diag, np.zeros((P, P)), diag], 1)
    q0, q1, keys = k, k + P, np.arange(2 * P)[None, :]

    def band(q, key):
        near = (key // 64 <= q // 64) & (key // 64 >= q // 64 - 1)
        return np.where(near, np.abs(q - key), FAR)

    dist = np.concatenate([band(q0, keys[:, :P]), band(q1, keys)], 1)
    return np.concatenate([ident, tri, np.ones((P, P)), causal, dist], 1).astype(np.float32)


def trunk(nc, x_in, w_gate, w_up, w_down, norm_g, a_w_in, a_b_f, a_w_o, kv_norm_g, b_w_kv, b_w_q,
          b_sinks, b_w_o, tables, out):
    ctx = ExitStack()
    with ctx:
        def sb(name, shape, dt=F32):
            return ctx.enter_context(nc.sbuf_tensor(name, shape, dt))

        def sem(name):
            return ctx.enter_context(nc.semaphore(name))

        w_raw = sb("w_raw", [P, RING, 4, COLS])
        w_hi = sb("w_hi", [P, RING, 4, COLS], F32R)
        w_lo = sb("w_lo", [P, RING, 4, COLS], F32R)
        x = sb("x", [P, NB, D])
        xg = sb("xg", [P, NB, D])
        squares = sb("squares", [P, D], mybir.dt.bfloat16)
        gains = sb("gains", [P, GAINS, D])
        xt_hi = sb("xt_hi", [P, 2, DC, NB * P], F32R)
        xt_lo = sb("xt_lo", [P, 2, DC, NB * P], F32R)
        ht_hi = sb("ht_hi", [P, 2, NB * P], F32R)
        ht_lo = sb("ht_lo", [P, 2, NB * P], F32R)
        zeros = sb("zeros", [P, COLS], F32R)
        q_rows = sb("q_rows", [P, NB, COLS])
        silu = q_rows[:, 0, :].rearrange("p (t f) -> p t f", t=NB)
        hid = q_rows[:, 1, :].rearrange("p (t f) -> p t f", t=NB)
        k_rows = sb("k_rows", [P, NB, COLS])
        v_rows = sb("v_rows", [P, NB, D])
        q_t = sb("q_t", [P, PAIRS, NB * P])
        k_t = sb("k_t", [P, PAIRS, NB * P])
        probs = sb("probs", [P, 3, 2, SEG])
        probs_t = sb("probs_t", [P, 2, 2, SEG])
        decay = sb("decay", [P, 2, SEG])
        table = sb("table", [P, 3 * P + 2 * SEG])
        ident, tri, ones = table[:, 0:P], table[:, P:2 * P], table[:, 2 * P:3 * P]
        tri_ones = table[:, P:3 * P]
        causal, dist = table[:, 3 * P:3 * P + SEG], table[:, 3 * P + SEG:]
        wf_raw = sb("wf_raw", [P, DC, H])
        wf_hi = sb("wf_hi", [P, DC, P], F32R)
        wf_lo = sb("wf_lo", [P, DC, P], F32R)
        f_rows = sb("f_rows", [H, NB * P])
        fz = sb("fz", [P, 4, NB, H])
        logf = sb("logf", [P, NB, H])
        c_tok = sb("c_tok", [P, NB, H])
        c_t = sb("c_t", [H, NB * P])
        bf = sb("bf", [P, H])
        sinks = sb("sinks", [P, H])
        half_power = sb("half_power", [P, 1])
        ss_y = sb("ss_y", [P, NB])
        ss_x = sb("ss_x", [P, NB])
        r_y = sb("r_y", [P, NB])
        r_x = sb("r_x", [P, NB])
        r_tmp = sb("r_tmp", [P, 2, NB])
        mx = sb("mx", [P, 2, 2, NB])
        neg_mx = sb("neg_mx", [P, 2, 2, NB])
        sums = sb("sums", [P, 2, 2, NB])
        sink_d = sb("sink_d", [P, 2, 2, NB])
        sink_e = sb("sink_e", [P, 2, 2, NB])
        recip = sb("recip", [P, 2, 2, NB])
        ps = ctx.enter_context(nc.psum_tensor("ps", [P, 8, 512], F32))

        raw_landed = [sem(f"raw_landed{i}") for i in range(RING)]
        hi_ready, lo_ready, unit_used = sem("hi_ready"), sem("lo_ready"), sem("unit_used")
        x_landed, table_landed, small_landed = sem("x_landed"), sem("table_landed"), sem("small_landed")
        gain_landed = [sem(f"gain_landed{i}") for i in range(GAINS)]
        gain_used = sem("gain_used")
        gu0_ready = sem("gu0_ready")
        silu_ready, hid_ready, ht_raw = sem("silu_ready"), sem("hid_ready"), sem("ht_raw")
        ht_hi_ready, ht_ready, y0_ready = sem("ht_hi_ready"), sem("ht_ready"), sem("y0_ready")
        sq_y_ready, sq_x_ready, r_y_ready, r_x_ready = (sem("sq_y_ready"), sem("sq_x_ready"),
                                                        sem("r_y_ready"), sem("r_x_ready"))
        x_ready, xg_ready, xt_raw = sem("x_ready"), sem("xg_ready"), sem("xt_raw")
        xt_hi_ready, xt_ready = sem("xt_hi_ready"), sem("xt_ready")
        pool_step, dve_step, act_step = sem("pool_step"), sem("dve_step"), sem("act_step")
        zeros_ready, wf_hi_ready, wf_ready = sem("zeros_ready"), sem("wf_hi_ready"), sem("wf_ready")
        f_raw, f_rows_ready, f_t_raw, fz_ready, fe_ready = (sem("f_raw"), sem("f_rows_ready"), sem("f_t_raw"),
                                                            sem("fz_ready"), sem("fe_ready"))
        logf_ready, c_raw, c_ready = sem("logf_ready"), sem("c_raw"), sem("c_ready")
        act_evac, dve_evac, rows_t = sem("act_evac"), sem("dve_evac"), sem("rows_t")
        cb_raw, decay_ready, sc_raw, logits_done = (sem("cb_raw"), sem("decay_ready"), sem("sc_raw"),
                                                    sem("logits_done"))
        neg_mx_ready, exp_ready, probs_ready = sem("neg_mx_ready"), sem("exp_ready"), sem("probs_ready")
        pt_raw, pt_ready, ot_raw, ot_hi_ready, ot_ready = (sem("pt_raw"), sem("pt_ready"), sem("ot_raw"),
                                                           sem("ot_hi_ready"), sem("ot_ready"))
        out_done = sem("out_done")

        U_FFN = [0, 33 + 16, 33 + 16 + 33 + 2, 33 + 16 + 33 + 2 + 33 + 8]
        U_IN, U_AO = 33, 33 + 12
        U_KV = U_FFN[1] + 33
        U_Q, U_BO = U_FFN[2] + 33, U_FFN[2] + 33 + 4
        UNITS = U_FFN[3] + 33
        IN_COLS = [0, D, 2 * D, COLS, D + COLS, 2 * D + COLS]

        FFN_PREP = [0, 2, 4, 6]
        P_FOX, P_KV, P_SWA = 1, 3, 5
        VERSION = [0, 1, 2, 3, 3, 4, 5]
        GAIN_ROWS = [(0, 0), (0, 1), (0, 2), (0, 3), (0, 4), (0, 5), None, (1, 0), (1, 1), (1, 2),
                     (1, 3), (1, 4), (1, 5)]
        PRE = [0, 2, 4, 6, 7, 9, 11]
        POST = [1, 3, 5, 8, 10, 12]

        ACT_EVACS = ["k0", "tk0", "k1", "tk1", "kv", "tkv", "tb0", "tb1"]
        DVE_EVACS = ["q0", "tq0", "v0", "q1", "tq1", "v1", "kv", "b0", "b1"]

        def act_evacs(name):
            return ACT_EVACS.index(name) + 1

        def dve_evacs(name):
            return DVE_EVACS.index(name) + 1

        ROWS_T = ["q0", "k0", "q1", "k1", "kv", "b0", "b1"]

        def landed(u, i=0):
            return DMAS * 16 * (u // RING + 1) + DMAS * 16 * i

        block = ctx.enter_context(nc.Block())

        @block.sync
        def _(sp):
            for t in range(NB):
                sp.dma_start(x[:, t, :], x_in[0, t * P:(t + 1) * P, :]).then_inc(x_landed, 16)

            def load(u, pieces, i=0):
                if u >= RING or not isinstance(i, int):
                    sp.wait_ge(lo_ready, u - RING + 1 + 3 * i)
                for dst, src in pieces:
                    sp.dma_start(dst, src).then_inc(raw_landed[u % RING], 16)

            def columns(u, w, col, half):
                rows = w[half * 4 * P:(half + 1) * 4 * P, col:col + COLS].rearrange("(k p) n -> p k n", p=P)
                load(u, [(w_raw[:, u % RING, 2 * n:2 * n + 2, :], rows[:, 2 * n:2 * n + 2, :]) for n in range(2)])

            def gate_up(u, l, j, half, step, i=0):
                rows = slice(half * 4 * P, (half + 1) * 4 * P)
                cols = bass.ds(step * FC, FC)
                load(u, [(w_raw[:, u % RING, :, n * FC:(n + 1) * FC],
                          w[l, j, rows, cols].rearrange("(k p) f -> p k f", p=P))
                         for n, w in enumerate((w_gate, w_up))], i)

            def down(u, l, j, step, i=0):
                load(u, [(w_raw[:, u % RING, 2 * n:2 * n + 2, :].rearrange("p a b -> p (a b)"),
                          w_down[l, j, bass.ds(step * FC + n * P, P), :]) for n in range(2)], i)

            def ffn(f):
                l, j, u = f // 2, f % 2, U_FFN[f]
                gate_up(u, l, j, 0, 0)
                gate_up(u + 1, l, j, 1, 0)
                gate_up(u + 2, l, j, 0, 1)
                gate_up(u + 3, l, j, 1, 1)
                down(u + 4, l, j, 0)
                with sp.Fori(1, STEPS - 1) as i:
                    gate_up(u + 2, l, j, 0, i + 1, i)
                    gate_up(u + 3, l, j, 1, i + 1, i)
                    down(u + 4, l, j, i, i)
                down(u + 32, l, j, STEPS - 1)

            ffn(0)
            for n, col in enumerate(IN_COLS):
                for half in range(2):
                    columns(U_IN + 2 * n + half, a_w_in[0], col, half)
            for n in range(4):
                columns(U_AO + n, a_w_o[0], (n // 2) * COLS, n % 2)
            ffn(1)
            for half in range(2):
                columns(U_KV + half, b_w_kv, 0, half)
            ffn(2)
            for n in range(4):
                columns(U_Q + n, b_w_q[0], (n // 2) * COLS, n % 2)
            for n in range(4):
                columns(U_BO + n, b_w_o[0], (n // 2) * COLS, n % 2)
            ffn(3)
            for t in range(NB):
                sp.wait_ge(x_ready, 6 * NB + t + 1)
                sp.dma_start(out[0, t * P:(t + 1) * P, :], x[:, t, :]).then_inc(out_done, 16)
            sp.wait_ge(out_done, 16 * NB)

        @block.gpsimd
        def _(pool):
            steps = [0]

            def chained(ins):
                steps[0] += 1
                ins.then_inc(pool_step, 1)
                pool.wait_ge(pool_step, steps[0])

            def load_gain(m):
                if m >= GAINS:
                    pool.wait_ge(gain_used, m - GAINS + 1)
                row = GAIN_ROWS[m]
                src = kv_norm_g if row is None else norm_g[row[0], row[1]]
                pool.dma_start(gains[:, m % GAINS, :], src.partition_broadcast(P)).then_inc(gain_landed[m % GAINS], 16)

            def reciprocal_rms(src, dst, ready, needed, n, halve):
                t = n % NB
                pool.wait_ge(needed, n + 1)
                f = 4.0 if halve else 1.0
                chained(nc.gpsimd.tensor_scalar(r_tmp[:, n % 2, t:t + 1], src[:, t:t + 1], f / D, f * EPS,
                                                ALU.mult, ALU.add))
                nc.gpsimd.tensor_tensor(dst[:, t:t + 1], r_tmp[:, n % 2, t:t + 1], half_power[:, :],
                                        ALU.pow).then_inc(ready, 1)

            for m in range(GAINS):
                load_gain(m)
            chained(nc.gpsimd.memset(half_power[:, :], -0.5))
            nc.gpsimd.memset(zeros[:, :].bitcast(F32), 0.0).then_inc(zeros_ready, 1)
            nc.gpsimd.memset(wf_hi[:, :, :].bitcast(F32), 0.0).then_inc(zeros_ready, 1)
            nc.gpsimd.memset(wf_lo[:, :, :].bitcast(F32), 0.0).then_inc(zeros_ready, 1)
            m = GAINS
            for b in range(7):
                if b:
                    for t in range(NB):
                        reciprocal_rms(ss_y, r_y, r_y_ready, sq_y_ready, NB * (b - 1) + t, b in (1, 3, 4, 6))
                if b < 6:
                    for t in range(NB):
                        reciprocal_rms(ss_x, r_x, r_x_ready, sq_x_ready, NB * b + t, False)
                while m < len(GAIN_ROWS) and m - GAINS < [1, 3, 5, 8, 10, 12, 13][b]:
                    load_gain(m)
                    m += 1

        @block.scalar
        def _(act):
            act.dma_start(table[:, :], tables).then_inc(table_landed, 16)
            act.dma_start(wf_raw[:, :, :], a_w_in[0, :, 3 * D:3 * D + H].rearrange("(k p) h -> p k h", p=P))\
               .then_inc(small_landed, 16)
            act.dma_start(bf[:, :], a_b_f[0].partition_broadcast(P)).then_inc(small_landed, 16)
            act.dma_start(sinks[:, :], b_sinks[0].partition_broadcast(P)).then_inc(small_landed, 16)

            def split(u, i=0):
                act.wait_ge(raw_landed[u % RING], landed(u, i))
                if u >= RING or not isinstance(i, int):
                    act.wait_ge(unit_used, u - RING + 1 + 3 * i)
                nc.scalar.activation(w_hi[:, u % RING], w_raw[:, u % RING], ACT.Copy).then_inc(hi_ready, 1)

            squared = []

            def square(src, dst, ready, value):
                if squared:
                    act.wait_ge(*squared[-1])
                squared.append((ready, value))
                nc.scalar.activation(squares[:, :], src, ACT.Square, accum_out=dst).then_inc(ready, 1)

            def square_x(version):
                for t in range(NB):
                    act.wait_ge(x_ready, NB * version + t + 1)
                    square(x[:, t, :], ss_x[:, t:t + 1], sq_x_ready, NB * version + t + 1)

            def square_y(b, last_unit):
                act.wait_ge(y0_ready, b + 1)
                square(ps[:, Y:Y + 2, :].rearrange("p a b -> p (a b)"), ss_y[:, 0:1], sq_y_ready, NB * b + 1)
                act.wait_ge(unit_used, last_unit + 1)
                square(ps[:, Y + 2:Y + 4, :].rearrange("p a b -> p (a b)"), ss_y[:, 1:2], sq_y_ready, NB * b + 2)

            def xt_parts(k):
                for n in range(2 * NB):
                    t, half = n // 2, n % 2
                    act.wait_ge(xt_raw, 2 * NB * k + n + 1)
                    nc.scalar.activation(xt_hi[:, k % 2, 4 * half:4 * half + 4, t * P:(t + 1) * P],
                                         ps[:, n, :].rearrange("p (c t) -> p c t", t=P),
                                         ACT.Copy).then_inc(xt_hi_ready, 1)

            def silu_step(f, u, n, i=0, first=False):
                for t in range(NB):
                    if t == 0:
                        act.wait_ge(gu0_ready, n + 1 + i)
                    else:
                        act.wait_ge(unit_used, u + 1 + 3 * i)
                    if first:
                        act.wait_ge(r_x_ready, NB * VERSION[FFN_PREP[f]] + t + 1)
                    if n > 0 or not isinstance(i, int):
                        act.wait_ge(hid_ready, NB * (n + i) - NB + t + 1)
                    nc.scalar.activation(silu[:, t, :], ps[:, GU[t], 0:FC], ACT.Silu,
                                         scale=r_x[:, t:t + 1]).then_inc(silu_ready, 1)

            def ht_part(n, i=0):
                act.wait_ge(ht_raw, n + 1 + i)
                nc.scalar.activation(ht_hi[:, :, :], ps[:, HT, :].rearrange("p (c t) -> p c t", c=2),
                                     ACT.Copy).then_inc(ht_hi_ready, 1)

            def ffn(f):
                u, n = U_FFN[f], STEPS * f
                split(u + 2)
                silu_step(f, u + 1, n, first=True)
                split(u + 3)
                ht_part(n)
                split(u + 4)
                with act.Fori(1, STEPS - 1) as i:
                    split(u + 2, i)
                    silu_step(f, u, n, i)
                    split(u + 3, i)
                    ht_part(n, i)
                    split(u + 4, i)
                split(u + 32)
                silu_step(f, u + 30, n + STEPS - 1)
                if f < 3:
                    split(u + 33)
                ht_part(n + STEPS - 1)
                if f < 3:
                    split(u + 34)
                square_y([0, 2, 3, 5][f], u + 32)

            def rows_scaled(dst, bank, t):
                return nc.scalar.activation(dst, ps[:, bank, :], ACT.Copy, scale=r_x[:, t:t + 1])

            def evac_k(g, proj, last_unit):
                banks = 4 + 2 * (proj % 2)
                act.wait_ge(unit_used, last_unit + 1)
                if g:
                    act.wait_ge(rows_t, ROWS_T.index("k0") + 1)
                for t in range(NB):
                    last = rows_scaled(k_rows[:, t, :], banks + t, t)
                last.then_inc(act_evac, 1)

            def evac_t(dst, which, g):
                act.wait_ge(rows_t, ROWS_T.index(which) + 1)
                for n in range(2):
                    last = nc.scalar.activation(dst[:, 4 * g + 2 * n:4 * g + 2 * n + 2, :],
                                                ps[:, 2 + n, :].rearrange("p (c t) -> p c t", c=2), ACT.Copy)
                last.then_inc(act_evac, 1)

            def exps(pair, windowed):
                b, s = pair % 2, pair % 3
                act.wait_ge(neg_mx_ready, pair + 1)
                for j in range(2):
                    for t in range(NB):
                        seg = probs[:, s, j, 0:P] if t == 0 else probs[:, s, j, P:SEG]
                        last = nc.scalar.activation(seg, seg, ACT.Exp, bias=neg_mx[:, b, j, t:t + 1],
                                                    accum_out=sums[:, b, j, t:t + 1])
                if windowed:
                    last = nc.scalar.activation(sink_e[:, b], sink_d[:, b], ACT.Exp)
                last.then_inc(exp_ready, 1)

            def evac_pt(pair):
                act.wait_ge(pt_raw, pair + 1)
                if pair >= 2:
                    act.wait_ge(ot_raw, pair - 1)
                for j in range(2):
                    last = nc.scalar.activation(probs_t[:, pair % 2, j, :], ps[:, PTB[j], 0:SEG], ACT.Copy)
                last.then_inc(pt_ready, 1)

            def ot_part(pair):
                act.wait_ge(ot_raw, pair + 1)
                nc.scalar.activation(xt_hi[:, 0, pair % PAIRS, :], ps[:, OT, 0:NB * P], ACT.Copy)\
                  .then_inc(ot_hi_ready, 1)

            def attention(first, windowed):
                exps(first, windowed)
                for pair in range(first, first + PAIRS):
                    if pair + 1 < first + PAIRS:
                        exps(pair + 1, windowed)
                    evac_pt(pair)
                    ot_part(pair)

            split(0)
            split(1)
            act.wait_ge(small_landed, 48)
            act.wait_ge(zeros_ready, 3)
            nc.scalar.activation(wf_hi[:, :, 0:H], wf_raw[:, :, :], ACT.Copy).then_inc(wf_hi_ready, 1)
            xt_parts(0)
            square_x(0)
            ffn(0)

            xt_parts(P_FOX)
            square_x(1)
            split(U_IN + 2)
            act.wait_ge(f_raw, 1)
            nc.scalar.activation(f_rows[:, :], ps[0:H, 0, 0:NB * P], ACT.Copy).then_inc(f_rows_ready, 1)
            act.wait_ge(fz_ready, 1)
            nc.scalar.activation(fz[:, 2], fz[:, 1], ACT.Exp).then_inc(act_step, 1)
            act.wait_ge(act_step, 1)
            nc.scalar.activation(fz[:, 3], fz[:, 2], ACT.Ln, bias=1.0).then_inc(fe_ready, 1)
            split(U_IN + 3)
            act.wait_ge(c_raw, 1)
            nc.scalar.activation(c_t[:, :], ps[0:H, 1, 0:NB * P], ACT.Copy)
            nc.scalar.activation(c_tok[:, :, :], ps[:, 1, NB * P:NB * P + NB * H].rearrange("p (t h) -> p t h", h=H),
                                 ACT.Copy).then_inc(c_ready, 1)
            split(U_IN + 4)
            evac_k(0, 1, U_IN + 3)
            split(U_IN + 5)
            split(U_IN + 6)
            evac_t(k_t, "k0", 0)
            split(U_IN + 7)
            split(U_IN + 8)
            split(U_IN + 9)
            split(U_IN + 10)
            evac_k(1, 4, U_IN + 9)
            split(U_IN + 11)
            split(U_AO)
            evac_t(k_t, "k1", 1)
            split(U_AO + 1)
            attention(0, False)
            split(U_AO + 2)
            split(U_AO + 3)
            split(U_FFN[1])
            split(U_FFN[1] + 1)
            square_y(1, U_AO + 3)
            xt_parts(2)
            square_x(2)
            ffn(1)

            xt_parts(P_KV)
            square_x(3)
            split(U_FFN[2])
            act.wait_ge(unit_used, U_KV + 2)
            act.wait_ge(r_x_ready, NB * VERSION[P_KV] + NB)
            for t in range(NB):
                for twin in range(2):
                    last = nc.scalar.activation(
                        k_rows[:, t, :].rearrange("p (h s d) -> p h s d", s=2, d=DH)[:, :, twin, :],
                        ps[:, 4 + t, 0:KVH * DH].rearrange("p (h d) -> p h d", d=DH), ACT.Copy,
                        scale=r_x[:, t:t + 1])
            last.then_inc(act_evac, 1)
            split(U_FFN[2] + 1)
            xt_parts(4)
            act.wait_ge(rows_t, ROWS_T.index("kv") + 1)
            for n in range(2):
                last = nc.scalar.activation(k_t[:, 2 * n:2 * n + 2, :],
                                            ps[:, 6 + n, :].rearrange("p (c t) -> p c t", c=2), ACT.Copy)
            last.then_inc(act_evac, 1)
            ffn(2)

            xt_parts(P_SWA)
            square_x(4)
            split(U_Q + 2)
            split(U_Q + 3)
            split(U_BO)
            evac_t(q_t, "b0", 0)
            split(U_BO + 1)
            evac_t(q_t, "b1", 1)
            attention(PAIRS, True)
            split(U_BO + 2)
            split(U_BO + 3)
            split(U_FFN[3])
            split(U_FFN[3] + 1)
            square_y(4, U_BO + 3)
            xt_parts(6)
            square_x(5)
            ffn(3)

        @block.vector
        def _(dve):
            steps = [0]

            def chained(ins):
                steps[0] += 1
                ins.then_inc(dve_step, 1)
                dve.wait_ge(dve_step, steps[0])

            def split(u, i=0):
                dve.wait_ge(hi_ready, u + 1 + 3 * i)
                nc.vector.tensor_tensor(w_lo[:, u % RING], w_raw[:, u % RING], w_hi[:, u % RING].bitcast(F32),
                                        ALU.subtract).then_inc(lo_ready, 1)

            def gain(m):
                dve.wait_ge(gain_landed[m % GAINS], 16 * (m // GAINS + 1))
                return gains[:, m % GAINS, :]

            def pregain(k, t):
                ins = nc.vector.tensor_tensor(xg[:, t, :], x[:, t, :], gain(PRE[k]), ALU.mult)
                ins.then_inc(xg_ready, 1)

            def post(b, k):
                for t in range(NB):
                    dve.wait_ge(r_y_ready, NB * b + t + 1)
                    g = gain(POST[b])
                    chained(nc.vector.scalar_tensor_tensor(
                        out=xg[:, t, :], in0=ps[:, Y + 2 * t:Y + 2 * t + 2, :].rearrange("p a b -> p (a b)"),
                        scalar=r_y[:, t:t + 1], in1=g, op0=ALU.mult, op1=ALU.mult))
                    nc.vector.tensor_tensor(x[:, t, :], x[:, t, :], xg[:, t, :], ALU.add).then_inc(x_ready, 1)
                    if k is not None:
                        dve.wait_ge(x_ready, NB * (b + 1) + t + 1)
                        pregain(k, t)

            def gains_used(n):
                dve.drain().then_inc(gain_used, n)

            def xt_parts(k):
                for n in range(2 * NB):
                    t, half = n // 2, n % 2
                    dve.wait_ge(xt_hi_ready, 2 * NB * k + n + 1)
                    cols = (slice(None), k % 2, slice(4 * half, 4 * half + 4), slice(t * P, (t + 1) * P))
                    nc.vector.tensor_tensor(xt_lo[cols], ps[:, n, :].rearrange("p (c t) -> p c t", t=P),
                                            xt_hi[cols].bitcast(F32), ALU.subtract).then_inc(xt_ready, 1)

            def hid_step(n, i=0):
                for t in range(NB):
                    dve.wait_ge(silu_ready, NB * n + t + 1 + NB * i)
                    if not (isinstance(i, int) and n == 0):
                        dve.wait_ge(ht_raw, n + i)
                    nc.vector.scalar_tensor_tensor(out=hid[:, t, :], in0=ps[:, GU[t], FC:2 * FC],
                                                   scalar=r_x[:, t:t + 1], in1=silu[:, t, :], op0=ALU.mult,
                                                   op1=ALU.mult).then_inc(hid_ready, 1)

            def ht_part(n, i=0):
                dve.wait_ge(ht_hi_ready, n + 1 + i)
                nc.vector.tensor_tensor(ht_lo[:, :, :], ps[:, HT, :].rearrange("p (c t) -> p c t", c=2),
                                        ht_hi[:, :, :].bitcast(F32), ALU.subtract).then_inc(ht_ready, 1)

            def ffn(f):
                u, n = U_FFN[f], STEPS * f
                split(u + 2)
                hid_step(n)
                split(u + 3)
                ht_part(n)
                split(u + 4)
                with dve.Fori(1, STEPS - 1) as i:
                    split(u + 2, i)
                    hid_step(n, i)
                    split(u + 3, i)
                    ht_part(n, i)
                    split(u + 4, i)
                split(u + 32)
                hid_step(n + STEPS - 1)
                if f < 3:
                    split(u + 33)
                ht_part(n + STEPS - 1)
                if f < 3:
                    split(u + 34)

            def rows(dst, proj, last_unit, width=None, scale=1.0, reader=None):
                banks = 4 + 2 * (proj % 2)
                dve.wait_ge(unit_used, last_unit + 1)
                if reader is not None:
                    dve.wait_ge(rows_t, ROWS_T.index(reader) + 1)
                for t in range(NB):
                    src = ps[:, banks + t, :] if width is None else ps[:, banks + t, COLS - width:COLS]
                    last = nc.vector.tensor_scalar(dst(t), src, r_x[:, t:t + 1], scale, ALU.mult, ALU.mult)
                last.then_inc(dve_evac, 1)

            def logits(pair, windowed):
                p, b, s = pair % PAIRS, pair % 2, pair % 3
                if not windowed:
                    dve.wait_ge(cb_raw, p + 1)
                    spread = ps[:, CB, :].rearrange("p (h s) -> p h s", h=2)
                    for cols, src in ((slice(0, P), slice(0, P)), (slice(P, SEG), slice(0, 2 * P))):
                        width = cols.stop - cols.start
                        last = nc.vector.scalar_tensor_tensor(
                            out=decay[:, :, cols], in0=spread[:, :, src], scalar=-1.0,
                            in1=causal[:, cols].unsqueeze(1).to_broadcast([P, 2, width]), op0=ALU.mult, op1=ALU.add)
                    last.then_inc(decay_ready, 1)
                    dve.wait_ge(decay_ready, p + 1)
                dve.wait_ge(sc_raw, pair + 1)
                if pair >= 3:
                    dve.wait_ge(pt_raw, pair - 2)
                for j in range(2):
                    h = 2 * p + j
                    if windowed:
                        slope = float(np.float32(2.0) ** np.float32(-8.0 * (h + 1) / H))
                        last = nc.vector.scalar_tensor_tensor(out=probs[:, s, j, :], in0=dist, scalar=-slope,
                                                              in1=ps[:, SC[j], 0:SEG], op0=ALU.mult, op1=ALU.add)
                    else:
                        for t, cols in enumerate((slice(0, P), slice(P, SEG))):
                            last = nc.vector.scalar_tensor_tensor(
                                out=probs[:, s, j, cols], in0=ps[:, SC[j], cols], scalar=c_tok[:, t, h:h + 1],
                                in1=decay[:, j, cols], op0=ALU.add, op1=ALU.add)
                last.then_inc(logits_done, 1)
                dve.wait_ge(logits_done, pair + 1)
                nc.vector.reduce_max(mx[:, b, :, 0], probs[:, s, :, 0:P], AX.X)
                chained(nc.vector.reduce_max(mx[:, b, :, 1], probs[:, s, :, P:SEG], AX.X))
                if windowed:
                    sink = sinks[:, 2 * p:2 * p + 2].unsqueeze(2).to_broadcast([P, 2, NB])
                    chained(nc.vector.tensor_tensor(mx[:, b], mx[:, b], sink, ALU.max))
                    nc.vector.tensor_tensor(sink_d[:, b], sink, mx[:, b], ALU.subtract)
                nc.vector.tensor_scalar(neg_mx[:, b], mx[:, b], -1.0, None, ALU.mult).then_inc(neg_mx_ready, 1)

            def normalise(pair, windowed):
                b, s = pair % 2, pair % 3
                dve.wait_ge(exp_ready, pair + 1)
                if windowed:
                    chained(nc.vector.tensor_tensor(sums[:, b], sums[:, b], sink_e[:, b], ALU.add))
                chained(nc.vector.reciprocal(recip[:, b], sums[:, b]))
                for j in range(2):
                    for t in range(NB):
                        seg = probs[:, s, j, 0:P] if t == 0 else probs[:, s, j, P:SEG]
                        last = nc.vector.tensor_scalar(seg, seg, recip[:, b, j, t:t + 1], None, ALU.mult)
                last.then_inc(probs_ready, 1)

            def ot_part(pair):
                dve.wait_ge(ot_hi_ready, pair + 1)
                nc.vector.tensor_tensor(xt_lo[:, 0, pair % PAIRS, :], ps[:, OT, 0:NB * P],
                                        xt_hi[:, 0, pair % PAIRS, :].bitcast(F32), ALU.subtract).then_inc(ot_ready, 1)

            def attention(first, windowed):
                logits(first, windowed)
                logits(first + 1, windowed)
                for pair in range(first, first + PAIRS):
                    normalise(pair, windowed)
                    if pair + 2 < first + PAIRS:
                        logits(pair + 2, windowed)
                    ot_part(pair)

            split(0)
            split(1)
            dve.wait_ge(wf_hi_ready, 1)
            nc.vector.tensor_tensor(wf_lo[:, :, 0:H], wf_raw[:, :, :], wf_hi[:, :, 0:H].bitcast(F32),
                                    ALU.subtract).then_inc(wf_ready, 1)
            dve.wait_ge(x_landed, 16 * NB)
            for t in range(NB):
                pregain(0, t)
            gains_used(1)
            dve.drain().then_inc(x_ready, NB)
            xt_parts(0)
            ffn(0)

            post(0, P_FOX)
            gains_used(2)
            xt_parts(P_FOX)
            split(U_IN + 2)
            dve.wait_ge(f_t_raw, 1)
            dve.wait_ge(r_x_ready, NB * VERSION[P_FOX] + NB)
            f_tok = ps[:, 1, 0:NB * H].rearrange("p (t h) -> p t h", h=H)
            for t in range(NB):
                last = nc.vector.scalar_tensor_tensor(out=fz[:, 0, t, :], in0=f_tok[:, t, :], scalar=r_x[:, t:t + 1],
                                                      in1=bf[:, :], op0=ALU.mult, op1=ALU.add)
            chained(last)
            chained(nc.vector.scalar_tensor_tensor(out=fz[:, 1], in0=fz[:, 0], scalar=-1.0, in1=fz[:, 0],
                                                   op0=ALU.mult, op1=ALU.min))
            nc.vector.tensor_scalar(fz[:, 0], fz[:, 0], 0.0, None, ALU.min).then_inc(fz_ready, 1)
            dve.wait_ge(fz_ready, 1)
            dve.wait_ge(fe_ready, 1)
            nc.vector.tensor_tensor(logf[:, :, :], fz[:, 0], fz[:, 3], ALU.subtract).then_inc(logf_ready, 1)
            split(U_IN + 3)

            def q_rows_of(t):
                return q_rows[:, t, :]

            def evac_t(dst, which, g):
                dve.wait_ge(rows_t, ROWS_T.index(which) + 1)
                for n in range(2):
                    last = nc.vector.tensor_copy(dst[:, 4 * g + 2 * n:4 * g + 2 * n + 2, :],
                                                 ps[:, 2 + n, :].rearrange("p (c t) -> p c t", c=2))
                last.then_inc(dve_evac, 1)

            rows(q_rows_of, 0, U_IN + 1, scale=DH ** -0.5)
            split(U_IN + 4)
            split(U_IN + 5)
            evac_t(q_t, "q0", 0)
            split(U_IN + 6)
            rows(lambda t: v_rows[:, t, 0:COLS], 2, U_IN + 5)
            split(U_IN + 7)
            split(U_IN + 8)
            rows(q_rows_of, 3, U_IN + 7, scale=DH ** -0.5, reader="q0")
            split(U_IN + 9)
            split(U_IN + 10)
            split(U_IN + 11)
            evac_t(q_t, "q1", 1)
            split(U_AO)
            rows(lambda t: v_rows[:, t, COLS:D], 5, U_IN + 11)
            split(U_AO + 1)
            attention(0, False)
            split(U_AO + 2)
            split(U_AO + 3)
            split(U_FFN[1])
            split(U_FFN[1] + 1)
            post(1, 2)
            gains_used(2)
            xt_parts(2)
            ffn(1)

            post(2, P_KV)
            gains_used(2)
            xt_parts(P_KV)
            split(U_FFN[2])
            for t in range(NB):
                pregain(4, t)
            gains_used(1)
            dve.wait_ge(r_x_ready, NB * VERSION[P_KV] + NB)
            dve.wait_ge(act_evac, act_evacs("kv"))
            rows(lambda t: v_rows[:, t, 0:KVH * DH], 6, U_KV + 1, width=KVH * DH)
            split(U_FFN[2] + 1)
            xt_parts(4)
            ffn(2)

            post(3, P_SWA)
            gains_used(2)
            xt_parts(P_SWA)
            split(U_Q + 2)
            dve.wait_ge(r_x_ready, NB * VERSION[P_SWA] + NB)
            rows(q_rows_of, 8, U_Q + 1, scale=DH ** -0.5)
            split(U_Q + 3)
            split(U_BO)
            rows(q_rows_of, 9, U_Q + 3, scale=DH ** -0.5, reader="b0")
            split(U_BO + 1)
            attention(PAIRS, True)
            split(U_BO + 2)
            split(U_BO + 3)
            split(U_FFN[3])
            split(U_FFN[3] + 1)
            post(4, 6)
            gains_used(2)
            xt_parts(6)
            ffn(3)
            post(5, None)

        @block.tensor
        def _(pe):
            def transpose_x(k):
                for t in range(NB):
                    pe.wait_ge(xg_ready, NB * k + t + 1)
                    for half in range(2):
                        for c in range(4):
                            last = nc.tensor.transpose(ps[:, 2 * t + half, c * P:(c + 1) * P],
                                                       xg[:, t, (4 * half + c) * P:(4 * half + c + 1) * P], ident)
                        last.then_inc(xt_raw, 1)

            def unit(u, parity, half, banks, first=None, block0_done=None, i=0):
                slot = u % RING
                pe.wait_ge(lo_ready, u + 1 + 3 * i)
                for t in range(NB):
                    if first is not None:
                        pe.wait_ge(xt_ready, 2 * NB * first + 2 * t + half + 1)
                    for k in range(4):
                        left = (slice(None), parity, 4 * half + k, slice(t * P, (t + 1) * P))
                        start, stop = half == 0 and k == 0, half == 1 and k == 3
                        nc.tensor.matmul(ps[:, banks[t], :], xt_hi[left], w_hi[:, slot, k, :], start=start, stop=False)
                        nc.tensor.matmul(ps[:, banks[t], :], xt_hi[left], w_lo[:, slot, k, :], start=False, stop=False)
                        last = nc.tensor.matmul(ps[:, banks[t], :], xt_lo[left], w_hi[:, slot, k, :], start=False,
                                                stop=stop)
                    if t == 0 and block0_done is not None:
                        last.then_inc(block0_done, 1)
                last.then_inc(unit_used, 1)

            def clear_y():
                for bank in range(Y, Y + 4):
                    nc.tensor.matmul(ps[:, bank, :], zeros[:, 0:P], zeros[:, :], start=True, stop=False,
                                     skip_group_check=True)

            def transpose_h(n, i=0):
                for t in range(NB):
                    pe.wait_ge(hid_ready, NB * n + t + 1 + NB * i)
                    for c in range(2):
                        last = nc.tensor.transpose(ps[:, HT, (2 * c + t) * P:(2 * c + t + 1) * P],
                                                   hid[:, t, c * P:(c + 1) * P], ident)
                last.then_inc(ht_raw, 1)

            def down(u, n, final=False, i=0):
                slot = u % RING
                pe.wait_ge(ht_ready, n + 1 + i)
                pe.wait_ge(lo_ready, u + 1 + 3 * i)
                for t in range(NB):
                    for c in range(2):
                        tokens = slice(t * P, (t + 1) * P)
                        for left, w in ((ht_hi, w_hi), (ht_hi, w_lo), (ht_lo, w_hi)):
                            for half in range(2):
                                stop = final and c == 1 and left is ht_lo
                                last = nc.tensor.matmul(ps[:, Y + 2 * t + half, :], left[:, c, tokens],
                                                        w[:, slot, 2 * c + half, :], start=False, stop=stop,
                                                        skip_group_check=True)
                    if t == 0 and final:
                        last.then_inc(y0_ready, 1)
                last.then_inc(unit_used, 1)

            def ffn(f):
                u, n, k = U_FFN[f], STEPS * f, FFN_PREP[f]
                unit(u, 0, 0, GU, first=k)
                unit(u + 1, 0, 1, GU, first=k, block0_done=gu0_ready)
                clear_y()
                with pe.Fori(0, STEPS - 1) as i:
                    transpose_h(n, i)
                    unit(u + 2, 0, 0, GU, i=i)
                    unit(u + 3, 0, 1, GU, block0_done=gu0_ready, i=i)
                    down(u + 4, n, i=i)
                transpose_h(n + STEPS - 1)
                down(u + 32, n + STEPS - 1, final=True)

            def projection(proj, u, prep, parity, free):
                banks = (4 + 2 * (proj % 2), 5 + 2 * (proj % 2))
                for s, value in free:
                    pe.wait_ge(s, value)
                unit(u, parity, 0, banks, first=prep)
                unit(u + 1, parity, 1, banks, first=prep)

            def transpose_rows(rows, evac, free, bank=2):
                for s, value in (evac, *free):
                    pe.wait_ge(s, value)
                for c in range(4):
                    for t in range(NB):
                        last = nc.tensor.transpose(ps[:, bank + c // 2, ((c % 2) * 2 + t) * P:((c % 2) * 2 + t + 1) * P],
                                                   rows[:, t, c * P:(c + 1) * P], ident)
                last.then_inc(rows_t, 1)

            def forget_gates():
                pe.wait_ge(wf_ready, 1)
                pe.wait_ge(xt_ready, 2 * NB * (P_FOX + 1))
                for c in range(DC):
                    for left, right in ((wf_hi, xt_hi), (wf_hi, xt_lo), (wf_lo, xt_hi)):
                        last = nc.tensor.matmul(ps[:, 0, 0:NB * P], left[:, c, :], right[:, P_FOX % 2, c, :],
                                                start=c == 0 and left is wf_hi and right is xt_hi,
                                                stop=c == DC - 1 and left is wf_lo)
                last.then_inc(f_raw, 1)

            def forget_tokens():
                pe.wait_ge(f_rows_ready, 1)
                for t in range(NB):
                    last = nc.tensor.transpose(ps[:, 1, t * H:(t + 1) * H], f_rows[:, t * P:(t + 1) * P],
                                               ident[0:H, 0:H])
                last.then_inc(f_t_raw, 1)

            def forget_sums():
                pe.wait_ge(logf_ready, 1)
                nc.tensor.matmul(ps[0:H, 1, 0:NB * P], logf[:, 0, :], tri_ones, start=True, stop=False)
                nc.tensor.matmul(ps[0:H, 1, P:NB * P], logf[:, 1, :], tri, start=False, stop=True)
                c = ps[:, 1, NB * P:NB * P + NB * H]
                nc.tensor.matmul(c[:, 0:H], tri, logf[:, 0, :], start=True, stop=True)
                nc.tensor.matmul(c[:, H:2 * H], ones, logf[:, 0, :], start=True, stop=False)
                nc.tensor.matmul(c[:, H:2 * H], tri, logf[:, 1, :], start=False, stop=True).then_inc(c_raw, 1)

            def spread_sums(p):
                if p:
                    pe.wait_ge(decay_ready, p)
                for j in range(2):
                    h = 2 * p + j
                    last = nc.tensor.matmul(ps[:, CB, j * NB * P:(j + 1) * NB * P],
                                            ident[0:H, h:h + 1].to_broadcast([H, P]), c_t[:, :], start=True, stop=True)
                last.then_inc(cb_raw, 1)

            def scores(pair, windowed):
                p = pair % PAIRS
                if pair:
                    pe.wait_ge(logits_done, pair)
                for j in range(2):
                    heads = slice(j * DH, (j + 1) * DH)
                    keys = k_t[heads, p // 2 if windowed else p, :]
                    nc.tensor.matmul(ps[:, SC[j], 0:P], q_t[heads, p, 0:P], keys[:, 0:P], start=True, stop=True)
                    last = nc.tensor.matmul(ps[:, SC[j], P:SEG], q_t[heads, p, P:NB * P], keys, start=True, stop=True)
                last.then_inc(sc_raw, 1)

            def transpose_probs(pair):
                pe.wait_ge(probs_ready, pair + 1)
                if pair:
                    pe.wait_ge(pt_ready, pair)
                for j in range(2):
                    for n in range(3):
                        last = nc.tensor.transpose(ps[:, PTB[j], n * P:(n + 1) * P],
                                                   probs[:, pair % 3, j, n * P:(n + 1) * P], ident)
                last.then_inc(pt_raw, 1)

            def values(pair, windowed):
                p = pair % PAIRS
                pe.wait_ge(pt_ready, pair + 1)
                if pair:
                    pe.wait_ge(ot_ready, pair)
                for j in range(2):
                    h = (2 * p + j) // 4 if windowed else 2 * p + j
                    v = v_rows[:, :, h * DH:(h + 1) * DH]
                    o = ps[j * DH:(j + 1) * DH, OT, 0:NB * P]
                    pt = probs_t[:, pair % 2, j, :]
                    nc.tensor.matmul(o, v[:, 0, :], pt[:, 0:2 * P], start=True, stop=False)
                    last = nc.tensor.matmul(o[:, P:2 * P], v[:, 1, :], pt[:, 2 * P:SEG], start=False, stop=True)
                last.then_inc(ot_raw, 1)

            def attention(first, windowed):
                for pair in (first, first + 1):
                    if not windowed:
                        spread_sums(pair)
                    scores(pair, windowed)
                for pair in range(first, first + PAIRS):
                    transpose_probs(pair)
                    if pair + 2 < first + PAIRS:
                        if not windowed:
                            spread_sums(pair + 2)
                        scores(pair + 2, windowed)
                    values(pair, windowed)

            def output(u, first):
                pe.wait_ge(ot_ready, first + PAIRS)
                for n in range(2):
                    for half in range(2):
                        unit(u + 2 * n + half, 0, half, (Y + n, Y + 2 + n),
                             block0_done=y0_ready if n and half else None)

            pe.wait_ge(table_landed, 16)
            pe.wait_ge(zeros_ready, 3)
            transpose_x(0)
            ffn(0)

            transpose_x(P_FOX)
            forget_gates()
            projection(0, U_IN, P_FOX, 1, [])
            forget_tokens()
            projection(1, U_IN + 2, None, 1, [])
            forget_sums()
            transpose_rows(q_rows, (dve_evac, dve_evacs("q0")), [])
            projection(2, U_IN + 4, None, 1, [(dve_evac, dve_evacs("q0"))])
            transpose_rows(k_rows, (act_evac, act_evacs("k0")), [(dve_evac, dve_evacs("tq0"))])
            projection(3, U_IN + 6, None, 1, [(act_evac, act_evacs("k0"))])
            projection(4, U_IN + 8, None, 1, [(dve_evac, dve_evacs("v0"))])
            transpose_rows(q_rows, (dve_evac, dve_evacs("q1")), [(act_evac, act_evacs("tk0"))])
            projection(5, U_IN + 10, None, 1, [(dve_evac, dve_evacs("q1"))])
            transpose_rows(k_rows, (act_evac, act_evacs("k1")), [(dve_evac, dve_evacs("tq1"))])
            pe.wait_ge(c_ready, 1)
            pe.wait_ge(act_evac, act_evacs("tk1"))
            pe.wait_ge(dve_evac, dve_evacs("v1"))
            attention(0, False)
            output(U_AO, 0)
            transpose_x(2)
            ffn(1)

            transpose_x(P_KV)
            projection(6, U_KV, P_KV, 1, [])
            transpose_x(4)
            transpose_rows(k_rows, (act_evac, act_evacs("kv")), [], bank=6)
            pe.wait_ge(dve_evac, dve_evacs("kv"))
            pe.wait_ge(act_evac, act_evacs("tkv"))
            ffn(2)

            transpose_x(P_SWA)
            projection(8, U_Q, P_SWA, 1, [])
            projection(9, U_Q + 2, None, 1, [])
            transpose_rows(q_rows, (dve_evac, dve_evacs("b0")), [])
            transpose_rows(q_rows, (dve_evac, dve_evacs("b1")), [(act_evac, act_evacs("tb0"))])
            pe.wait_ge(act_evac, act_evacs("tb1"))
            attention(PAIRS, True)
            output(U_BO, PAIRS)
            transpose_x(6)
            ffn(3)


_INS = ["x", "ffn_w_gate", "ffn_w_up", "ffn_w_down", "norm_g", "a_w_in", "a_b_f", "a_w_o", "kv_norm_g", "b_w_kv",
        "b_w_q", "b_sinks", "b_w_o"]
_OUTS = [((1, NB * P, D), "float32")]


def kernel(**inputs):
    import numpy as _np
    import concourse.bacc as _bacc
    from concourse import mybir as _mybir
    from concourse.bass_utils import run_bass_kernel_spmd as _run

    nc = _bacc.Bacc("TRN2", target_bir_lowering=False, num_devices=1)
    arrays, args = {}, []
    for name in [*_INS, "tables"]:
        a = _np.ascontiguousarray(constants() if name == "tables" else inputs[name])
        arrays[f"in_{name}_dram"] = a
        args.append(nc.dram_tensor(f"in_{name}_dram", a.shape, _mybir.dt.from_np(a.dtype), kind="ExternalInput").ap())
    for i, (shape, dtype) in enumerate(_OUTS):
        dt = _mybir.dt.from_np(_np.dtype(dtype))
        args.append(nc.dram_tensor(f"out_{i}_dram", shape, dt, kind="ExternalOutput").ap())
    trunk(nc, *args)
    r = _run(nc, [arrays], core_ids=[0])
    return r.results[0]["out_0_dram"]
```

```python
from contextlib import ExitStack

import numpy as np

import concourse.bass as bass
from concourse import mybir

F32 = mybir.dt.float32
F32R = mybir.dt.float32r
ALU = mybir.AluOpType
ACT = mybir.ActivationFunctionType
AX = mybir.AxisListType

P = 128
NB = 2
D = 1024
DC = D // P
F = 2816
FC = 256
STEPS = F // FC
DH = 64
H = D // DH
PAIRS = H // 2
KVH = 4
COLS = 512
RING = 3
DMAS = 2
EPS = 1e-6
SEG = 3 * P
MASKED = -1.0e38
FAR = 1.0e38
GAINS = 3

GU = (0, 1)
HT = 2
Y = 4
SC = (0, 1)
PTB = (2, 3)
OT = 4
CB = 6
V0_BANKS = (2, 3)
Q1_BANKS = (6, 7)
ROWS = (5, 7)


def constants():
    k, s = np.arange(P)[:, None], np.arange(P)[None, :]
    ident = np.eye(P)
    tri = k <= s
    diag = np.where(s <= k, 0.0, MASKED)
    causal = np.concatenate([diag, np.zeros((P, P)), diag], 1)
    q0, q1, keys = k, k + P, np.arange(2 * P)[None, :]

    def band(q, key):
        near = (key // 64 <= q // 64) & (key // 64 >= q // 64 - 1)
        return np.where(near, np.abs(q - key), FAR)

    dist = np.concatenate([band(q0, keys[:, :P]), band(q1, keys)], 1)
    return np.concatenate([ident, tri, np.ones((P, P)), causal, dist], 1).astype(np.float32)


def trunk(nc, x_in, w_gate, w_up, w_down, norm_g, a_w_in, a_b_f, a_w_o, kv_norm_g, b_w_kv, b_w_q,
          b_sinks, b_w_o, tables, out):
    ctx = ExitStack()
    with ctx:
        def sb(name, shape, dt=F32):
            return ctx.enter_context(nc.sbuf_tensor(name, shape, dt))

        def sem(name):
            return ctx.enter_context(nc.semaphore(name))

        w_raw = sb("w_raw", [P, RING, 4, COLS])
        w_hi = sb("w_hi", [P, RING, 4, COLS], F32R)
        w_lo = sb("w_lo", [P, RING, 4, COLS], F32R)
        x = sb("x", [P, NB, D])
        xg = sb("xg", [P, NB, D])
        squares = sb("squares", [P, D], mybir.dt.bfloat16)
        gains = sb("gains", [P, GAINS, D])
        xt_hi = sb("xt_hi", [P, 2, DC, NB * P], F32R)
        xt_lo = sb("xt_lo", [P, 2, DC, NB * P], F32R)
        ht_hi = sb("ht_hi", [P, 2, NB * P], F32R)
        ht_lo = sb("ht_lo", [P, 2, NB * P], F32R)
        ht_last_hi = sb("ht_last_hi", [P, 2, NB * P], F32R)
        ht_last_lo = sb("ht_last_lo", [P, 2, NB * P], F32R)
        zeros = sb("zeros", [P, COLS], F32R)
        rows = sb("rows", [P, NB, COLS])
        silu = rows[:, 0, :].rearrange("p (t f) -> p t f", t=NB)
        hid = rows[:, 1, :].rearrange("p (t f) -> p t f", t=NB)
        v_rows = sb("v_rows", [P, NB, D])
        q_t = sb("q_t", [P, PAIRS, NB * P])
        k_t = sb("k_t", [P, PAIRS, NB * P])
        probs = sb("probs", [P, 3, 2, SEG])
        probs_t = sb("probs_t", [P, 2, 2, SEG])
        decay = sb("decay", [P, 2, SEG])
        table = sb("table", [P, 3 * P + 2 * SEG])
        ident, tri, ones = table[:, 0:P], table[:, P:2 * P], table[:, 2 * P:3 * P]
        tri_ones = table[:, P:3 * P]
        causal, dist = table[:, 3 * P:3 * P + SEG], table[:, 3 * P + SEG:]
        wf_raw = sb("wf_raw", [P, DC, H])
        wf_hi = sb("wf_hi", [P, DC, P], F32R)
        wf_lo = sb("wf_lo", [P, DC, P], F32R)
        f_rows = sb("f_rows", [H, NB * P])
        fz = sb("fz", [P, 4, NB, H])
        logf = sb("logf", [P, NB, H])
        c_tok = sb("c_tok", [P, NB, H])
        c_t = sb("c_t", [H, NB * P])
        bf = sb("bf", [P, H])
        sinks = sb("sinks", [P, H])
        half_power = sb("half_power", [P, 1])
        unread = sb("unread", [P, 8])
        ss_y = sb("ss_y", [P, NB, 2])
        ss_x = sb("ss_x", [P, NB])
        r_y = sb("r_y", [P, NB])
        r_x = sb("r_x", [P, NB])
        r_tmp = sb("r_tmp", [P, 2, NB])
        mx = sb("mx", [P, 2, 2, NB])
        neg_mx = sb("neg_mx", [P, 2, 2, NB])
        sums = sb("sums", [P, 2, 2, NB])
        sink_d = sb("sink_d", [P, 2, 2, NB])
        sink_e = sb("sink_e", [P, 2, 2, NB])
        recip = sb("recip", [P, 2, 2, NB])
        ps = ctx.enter_context(nc.psum_tensor("ps", [P, 8, 512], F32))

        raw_landed = [sem(f"raw_landed{i}") for i in range(RING)]
        hi_ready, lo_ready, unit_used = sem("hi_ready"), sem("lo_ready"), sem("unit_used")
        x_landed = [sem(f"x_landed{t}") for t in range(NB)]
        gain_landed = [sem(f"gain_landed{i}") for i in range(GAINS)]
        ident_landed, table_landed, small_landed = sem("ident_landed"), sem("table_landed"), sem("small_landed")
        out_done = sem("out_done")
        zeros_ready, wf_hi_ready, wf_ready = sem("zeros_ready"), sem("wf_hi_ready"), sem("wf_ready")
        pool_step, dve_step, act_step = sem("pool_step"), sem("dve_step"), sem("act_step")
        sq_y_ready, r_y_ready, sq_x_ready, r_x_ready = (sem("sq_y_ready"), sem("r_y_ready"), sem("sq_x_ready"),
                                                        sem("r_x_ready"))
        x_ready, xg_ready, xt_raw = sem("x_ready"), sem("xg_ready"), sem("xt_raw")
        xt_hi_ready, xt_ready = sem("xt_hi_ready"), sem("xt_ready")
        gu0_ready, silu_ready, hid_ready, ht_raw = (sem("gu0_ready"), sem("silu_ready"), sem("hid_ready"),
                                                    sem("ht_raw"))
        ht_hi_ready, ht_ready, y0_ready = sem("ht_hi_ready"), sem("ht_ready"), sem("y0_ready")
        f_raw, f_rows_ready, f_t_raw, fz_ready, fe_ready = (sem("f_raw"), sem("f_rows_ready"), sem("f_t_raw"),
                                                            sem("fz_ready"), sem("fe_ready"))
        logf_ready, c_raw, c_ready = sem("logf_ready"), sem("c_raw"), sem("c_ready")
        rows_act, rows_dve, rows_t = sem("rows_act"), sem("rows_dve"), sem("rows_t")
        heads_act, heads_dve = sem("heads_act"), sem("heads_dve")
        cb_raw, decay_ready, sc_raw, logits_done = (sem("cb_raw"), sem("decay_ready"), sem("sc_raw"),
                                                    sem("logits_done"))
        neg_mx_ready, exp_ready, probs_ready = sem("neg_mx_ready"), sem("exp_ready"), sem("probs_ready")
        pt_raw, pt_ready, ot_raw, ot_hi_ready, ot_ready = (sem("pt_raw"), sem("pt_ready"), sem("ot_raw"),
                                                           sem("ot_hi_ready"), sem("ot_ready"))

        N_FFN, N_FOX, N_KV, N_SWA = 3 * STEPS, 16, 2, 8
        U_FFN0 = 0
        U_FOX = U_FFN0 + N_FFN
        U_FFN1 = U_FOX + N_FOX
        U_KV = U_FFN1 + N_FFN
        U_FFN2 = U_KV + N_KV
        U_SWA = U_FFN2 + N_FFN
        U_FFN3 = U_SWA + N_SWA
        U_FFN = [U_FFN0, U_FFN1, U_FFN2, U_FFN3]
        QK = [0, 4, 6, 10]
        V = [2, 8]
        F_OUT, S_OUT = 12, 4
        ROW_ORDER = ["qk0", "v0", "qk1", "qk2", "v1", "qk3", "kv", "q0", "q1"]
        TURN_ORDER = ["qk0", "qk1", "qk2", "qk3", "kv", "q0", "q1"]

        FFN_PREP = [0, 2, 4, 6]
        P_FOX, P_KV, P_SWA = 1, 3, 5
        VERSION = [0, 1, 2, 3, 3, 4, 5]
        GAIN_ROWS = [(0, 0), (0, 1), (0, 2), (0, 3), (0, 4), (0, 5), None, (1, 0), (1, 1), (1, 2), (1, 3), (1, 4),
                     (1, 5)]
        PRE = [0, 2, 4, 6, 7, 9, 11]
        POST = [1, 3, 5, 8, 10, 12]
        SUBLAYERS = len(POST)
        WEIGHT = [4.0, 1.0, 4.0, 4.0, 1.0, 4.0]
        QS = 2 * NB

        def made(order, name):
            return order.index(name) + 1

        def ot_bank(pair):
            last = pair % PAIRS - (PAIRS - 2)
            return OT if last < 0 else SC[last]

        def looped(i):
            return not isinstance(i, int)

        block = ctx.enter_context(nc.Block())

        @block.sync
        def _(sp):
            def load_gain(m):
                before = m - GAINS
                if before >= 0 and before in PRE:
                    sp.wait_ge(xg_ready, QS * (PRE.index(before) + 1))
                elif before >= 0:
                    sp.wait_ge(x_ready, QS * (POST.index(before) + 1))
                row = GAIN_ROWS[m]
                src = kv_norm_g if row is None else norm_g[row[0], row[1]]
                sp.dma_start(gains[:, m % GAINS, :], src.partition_broadcast(P)).then_inc(gain_landed[m % GAINS], 16)

            def load(u, pieces, i=0):
                if u >= RING or looped(i):
                    sp.wait_ge(lo_ready, u - RING + 1 + 3 * i)
                for dst, src in pieces:
                    sp.dma_start(dst, src).then_inc(raw_landed[u % RING], 16)

            def columns(u, w, cols, half):
                width = COLS // len(cols)
                load(u, [(w_raw[:, u % RING, :, n * width:(n + 1) * width],
                          w[half * 4 * P:(half + 1) * 4 * P, col:col + width].rearrange("(k p) n -> p k n", p=P))
                         for n, col in enumerate(cols)])

            def gate_up(u, l, j, half, step, i=0):
                rws = slice(half * 4 * P, (half + 1) * 4 * P)
                cols = bass.ds(step * FC, FC)
                load(u, [(w_raw[:, u % RING, :, n * FC:(n + 1) * FC],
                          w[l, j, rws, cols].rearrange("(k p) f -> p k f", p=P))
                         for n, w in enumerate((w_gate, w_up))], i)

            def down(u, l, j, step, i=0):
                load(u, [(w_raw[:, u % RING, 2 * n:2 * n + 2, :].rearrange("p a b -> p (a b)"),
                          w_down[l, j, bass.ds(step * FC + n * P, P), :]) for n in range(2)], i)

            def ffn(f, next_gains):
                l, j, u = f // 2, f % 2, U_FFN[f]
                gate_up(u, l, j, 0, 0)
                gate_up(u + 1, l, j, 1, 0)
                gate_up(u + 2, l, j, 0, 1)
                gate_up(u + 3, l, j, 1, 1)
                down(u + 4, l, j, 0)
                for m in next_gains:
                    load_gain(m)
                with sp.Fori(1, STEPS - 1) as i:
                    gate_up(u + 2, l, j, 0, i + 1, i)
                    gate_up(u + 3, l, j, 1, i + 1, i)
                    down(u + 4, l, j, i, i)
                down(u + 32, l, j, STEPS - 1)

            def output_projection(u, w):
                for n in range(4):
                    col = COLS * (1 - n % 2)
                    columns(u + n, w, [col, col + COLS // 2], n // 2)

            for t in range(NB):
                sp.dma_start(x[:, t, :], x_in[0, t * P:(t + 1) * P, :]).then_inc(x_landed[t], 16)
                if t == 0:
                    load_gain(0)
            ffn(0, [1, 2])
            fox_units = sorted([(QK[g], [g * 2 * P, D + g * 2 * P]) for g in range(4)]
                               + [(V[g], [2 * D + g * COLS, 2 * D + g * COLS + COLS // 2]) for g in range(2)])
            for u, cols in fox_units:
                for half in range(2):
                    columns(U_FOX + u + half, a_w_in[0], cols, half)
                if u == V[0]:
                    load_gain(3)
                    load_gain(4)
            output_projection(U_FOX + F_OUT, a_w_o[0])
            ffn(1, [5, 6, 7])
            for half in range(2):
                columns(U_KV + half, b_w_kv, [0, COLS // 2], half)
            ffn(2, [8, 9])
            for n in range(4):
                columns(U_SWA + n, b_w_q[0], [(n // 2) * COLS, (n // 2) * COLS + COLS // 2], n % 2)
            load_gain(10)
            load_gain(11)
            output_projection(U_SWA + S_OUT, b_w_o[0])
            ffn(3, [12])
            for t in range(NB):
                for half in range(2):
                    cols = slice(half * COLS, (half + 1) * COLS)
                    sp.wait_ge(x_ready, QS * (SUBLAYERS - 1) + 2 * t + half + 1)
                    sp.dma_start(out[0, t * P:(t + 1) * P, cols], x[:, t, cols]).then_inc(out_done, 16)
            sp.wait_ge(out_done, 16 * QS)

        @block.gpsimd
        def _(pool):
            steps = [0]

            def chained(ins):
                steps[0] += 1
                ins.then_inc(pool_step, 1)
                pool.wait_ge(pool_step, steps[0])

            def reciprocal_rms(sums_of, dst, ready, n):
                t = n % NB
                chained(sums_of(r_tmp[:, n % 2, t:t + 1]))
                nc.gpsimd.tensor_tensor(dst[:, t:t + 1], r_tmp[:, n % 2, t:t + 1], half_power[:, :],
                                        ALU.pow).then_inc(ready, 1)

            def rms_y(b, t):
                pool.wait_ge(sq_y_ready, QS * b + 2 * t + 2)
                reciprocal_rms(lambda dst: nc.gpsimd.tensor_scalar(dst, ss_y[:, t, 0:1], ss_y[:, t, 1:2],
                                                                   WEIGHT[b] * EPS, ALU.add, ALU.add),
                               r_y, r_y_ready, NB * b + t)

            def rms_x(version, t):
                pool.wait_ge(sq_x_ready, NB * version + t + 1)
                reciprocal_rms(lambda dst: nc.gpsimd.tensor_scalar(dst, ss_x[:, t:t + 1], 1.0 / D, EPS, ALU.mult,
                                                                   ALU.add),
                               r_x, r_x_ready, NB * version + t)

            chained(nc.gpsimd.memset(half_power[:, :], -0.5))
            nc.gpsimd.memset(zeros[:, :].bitcast(F32), 0.0).then_inc(zeros_ready, 1)
            nc.gpsimd.memset(wf_hi[:, :, :].bitcast(F32), 0.0).then_inc(zeros_ready, 1)
            nc.gpsimd.memset(wf_lo[:, :, :].bitcast(F32), 0.0).then_inc(zeros_ready, 1)
            for v in range(SUBLAYERS + 1):
                for t in range(NB if v else 0):
                    rms_y(v - 1, t)
                for t in range(NB if v < SUBLAYERS else 0):
                    rms_x(v, t)

        @block.scalar
        def _(act):
            act.dma_start(table[:, 0:P], tables[:, 0:P]).then_inc(ident_landed, 16)

            tables_loaded = [0]

            def load_table(func):
                n = tables_loaded[0]
                tables_loaded[0] += 1
                nc.scalar.activation(unread[:, n:n + 1], half_power[:, :], func)

            def split(u, i=0):
                act.wait_ge(raw_landed[u % RING], DMAS * 16 * (u // RING + 1) + DMAS * 16 * i)
                if u >= RING or looped(i):
                    act.wait_ge(unit_used, u - RING + 1 + 3 * i)
                nc.scalar.activation(w_hi[:, u % RING], w_raw[:, u % RING], ACT.Copy).then_inc(hi_ready, 1)

            squared = []

            def square(src, dst, ready, value, scale=1.0):
                if squared:
                    act.wait_ge(*squared[-1])
                squared.append((ready, value))
                nc.scalar.activation(squares[:, 0:src.shape[-1]], src, ACT.Square, scale=scale,
                                     accum_out=dst).then_inc(ready, 1)

            def square_y(b, t):
                for half in range(2):
                    square(ps[:, Y + 2 * t + half, :], ss_y[:, t, half:half + 1], sq_y_ready,
                           QS * b + 2 * t + half + 1, scale=float(np.sqrt(WEIGHT[b] / D)))

            def square_x(version):
                for t in range(NB):
                    if version == 0:
                        act.wait_ge(x_landed[t], 16)
                    else:
                        act.wait_ge(x_ready, QS * (version - 1) + 2 * t + 2)
                    square(x[:, t, :], ss_x[:, t:t + 1], sq_x_ready, NB * version + t + 1)

            def xt_parts(k, t):
                for half in range(2):
                    n = 2 * t + half
                    act.wait_ge(xt_raw, QS * k + n + 1)
                    nc.scalar.activation(xt_hi[:, k % 2, 4 * half:4 * half + 4, t * P:(t + 1) * P],
                                         ps[:, n, :].rearrange("p (c t) -> p c t", t=P),
                                         ACT.Copy).then_inc(xt_hi_ready, 1)

            def boundary(b, last_unit, k):
                act.wait_ge(y0_ready, b + 1)
                square_y(b, 0)
                if k is not None:
                    split(last_unit + 2)
                act.wait_ge(unit_used, last_unit + 1)
                if k is None:
                    square_y(b, 1)
                    return
                xt_parts(k, 0)
                square_y(b, 1)
                split(last_unit + 3)
                xt_parts(k, 1)
                square_x(VERSION[k])

            def silu_step(f, u, n, i=0, first=False):
                for t in range(NB):
                    if t == 0:
                        act.wait_ge(gu0_ready, n + 1 + i)
                    else:
                        act.wait_ge(unit_used, u + 1 + 3 * i)
                    if first:
                        act.wait_ge(r_x_ready, NB * VERSION[FFN_PREP[f]] + t + 1)
                    if n > 0 or looped(i):
                        act.wait_ge(hid_ready, NB * (n + i) - NB + t + 1)
                    nc.scalar.activation(silu[:, t, :], ps[:, GU[t], 0:FC], ACT.Silu,
                                         scale=r_x[:, t:t + 1]).then_inc(silu_ready, 1)

            def ht_part(n, i=0, dst=ht_hi):
                act.wait_ge(ht_raw, n + 1 + i)
                nc.scalar.activation(dst[:, :, :], ps[:, HT, :].rearrange("p (c t) -> p c t", c=2),
                                     ACT.Copy).then_inc(ht_hi_ready, 1)

            def ffn(f):
                u, n = U_FFN[f], STEPS * f
                silu_step(f, u + 1, n, first=True)
                split(u + 3)
                ht_part(n)
                split(u + 4)
                with act.Fori(1, STEPS - 1) as i:
                    split(u + 2, i)
                    silu_step(f, u, n, i)
                    split(u + 3, i)
                    ht_part(n, i)
                    split(u + 4, i)
                split(u + 32)
                silu_step(f, u + 30, n + STEPS - 1)
                if f < 3:
                    split(u + 33)
                ht_part(n + STEPS - 1, dst=ht_last_hi)

            def rows_out(last_unit, dst, bank=ROWS[0]):
                act.wait_ge(unit_used, last_unit + 1)
                act.wait_ge(r_x_ready, NB * VERSION[P_FOX if last_unit < U_FFN1 else P_SWA] + NB)
                nc.scalar.activation(dst, ps[:, bank, :], ACT.Copy, scale=r_x[:, 0:1]).then_inc(rows_act, 1)

            def heads_out(name, dst, scale):
                act.wait_ge(rows_t, made(TURN_ORDER, name))
                nc.scalar.activation(dst, ps[:, ROWS[0], :].rearrange("p (c t) -> p c t", c=2), ACT.Copy,
                                     scale=scale).then_inc(heads_act, 1)

            def exps(pair):
                b, s, windowed = pair % 2, pair % 3, pair >= PAIRS
                act.wait_ge(neg_mx_ready, pair + 1)
                for j in range(2):
                    for t, cols in enumerate((slice(0, P), slice(P, SEG))):
                        last = nc.scalar.activation(probs[:, s, j, cols], probs[:, s, j, cols], ACT.Exp,
                                                    bias=neg_mx[:, b, j, t:t + 1], accum_out=sums[:, b, j, t:t + 1])
                if windowed:
                    last = nc.scalar.activation(sink_e[:, b], sink_d[:, b], ACT.Exp)
                last.then_inc(exp_ready, 1)

            def probs_t_out(pair):
                act.wait_ge(pt_raw, pair + 1)
                if pair >= 2:
                    act.wait_ge(ot_raw, pair - 1)
                for j in range(2):
                    last = nc.scalar.activation(probs_t[:, pair % 2, j, :], ps[:, PTB[j], 0:SEG], ACT.Copy)
                last.then_inc(pt_ready, 1)

            def ot_part(pair):
                act.wait_ge(ot_raw, pair + 1)
                nc.scalar.activation(xt_hi[:, 0, pair % PAIRS, :], ps[:, ot_bank(pair), 0:NB * P], ACT.Copy)\
                  .then_inc(ot_hi_ready, 1)

            def qk_rows_out(g):
                rows_out(U_FOX + QK[g] + 1, rows[:, 0, :])

            def q_out(g):
                heads_out(f"qk{g}", q_t[:, 2 * g:2 * g + 2, :], DH ** -0.5)

            act.wait_ge(pool_step, 1)
            load_table(ACT.Silu)
            xt_parts(0, 0)
            xt_parts(0, 1)
            split(0)
            split(1)
            square_x(0)
            split(2)
            act.dma_start(table[:, P:], tables[:, P:]).then_inc(table_landed, 16)
            act.dma_start(wf_raw[:, :, :], a_w_in[0, :, 3 * D:3 * D + H].rearrange("(k p) h -> p k h", p=P))\
               .then_inc(small_landed, 16)
            act.dma_start(bf[:, :], a_b_f[0].partition_broadcast(P)).then_inc(small_landed, 16)
            act.dma_start(sinks[:, :], b_sinks[0].partition_broadcast(P)).then_inc(small_landed, 16)
            ffn(0)

            U = U_FOX
            act.wait_ge(small_landed, 48)
            act.wait_ge(zeros_ready, 3)
            nc.scalar.activation(wf_hi[:, :, 0:H], wf_raw[:, :, :], ACT.Copy).then_inc(wf_hi_ready, 1)
            boundary(0, U - 1, P_FOX)
            qk_rows_out(0)
            split(U + 3)
            act.wait_ge(f_raw, 1)
            nc.scalar.activation(f_rows[:, :], ps[0:H, 0, 0:NB * P], ACT.Copy).then_inc(f_rows_ready, 1)
            q_out(0)
            split(U + 4)
            act.wait_ge(fz_ready, 1)
            nc.scalar.activation(fz[:, 2], fz[:, 1], ACT.Exp).then_inc(act_step, 1)
            act.wait_ge(act_step, 1)
            nc.scalar.activation(fz[:, 3], fz[:, 2], ACT.Ln, bias=1.0).then_inc(fe_ready, 1)
            split(U + 5)
            act.wait_ge(c_raw, 1)
            nc.scalar.activation(c_t[:, :], ps[0:H, 1, 0:NB * P], ACT.Copy)
            nc.scalar.activation(c_tok[:, :, :], ps[:, 1, NB * P:NB * P + NB * H].rearrange("p (t h) -> p t h", h=H),
                                 ACT.Copy).then_inc(c_ready, 1)
            load_table(ACT.Exp)
            rows_out(U + V[0] + 1, v_rows[:, 0, 0:COLS], bank=V0_BANKS[0])
            split(U + 6)
            exps(0)
            probs_t_out(0)
            split(U + 7)
            exps(1)
            qk_rows_out(1)
            ot_part(0)
            q_out(1)
            probs_t_out(1)
            split(U + 8)
            exps(2)
            ot_part(1)
            probs_t_out(2)
            split(U + 9)
            exps(3)
            qk_rows_out(2)
            ot_part(2)
            q_out(2)
            probs_t_out(3)
            split(U + 10)
            exps(4)
            ot_part(3)
            probs_t_out(4)
            split(U + 11)
            rows_out(U + V[1] + 1, v_rows[:, 0, COLS:D])
            split(U + 12)
            exps(5)
            ot_part(4)
            probs_t_out(5)
            split(U + 13)
            qk_rows_out(3)
            ot_part(5)
            q_out(3)
            split(U + 14)
            exps(6)
            probs_t_out(6)
            exps(7)
            split(U + 15)
            ot_part(6)
            probs_t_out(7)
            split(U + 16)
            ot_part(7)
            load_table(ACT.Silu)
            boundary(1, U_FFN1 - 1, 2)
            ffn(1)

            boundary(2, U_KV - 1, P_KV)
            xt_parts(4, 0)
            split(U_FFN2 + 1)
            act.wait_ge(unit_used, U_KV + 2)
            act.wait_ge(r_x_ready, NB * VERSION[P_KV] + NB)
            for twin in range(2):
                nc.scalar.activation(rows[:, 0, :].rearrange("p (h s d) -> p h s d", s=2, d=DH)[:, :, twin, :],
                                     ps[:, ROWS[0], 0:KVH * DH].rearrange("p (h d) -> p h d", d=DH), ACT.Copy,
                                     scale=r_x[:, 0:1])
            nc.scalar.activation(v_rows[:, 0, 0:KVH * DH], ps[:, ROWS[0], KVH * DH:COLS], ACT.Copy,
                                 scale=r_x[:, 0:1]).then_inc(rows_act, 1)
            xt_parts(4, 1)
            split(U_FFN2 + 2)
            heads_out("kv", k_t[:, 0:2, :], 1.0)
            ffn(2)

            U = U_SWA
            boundary(3, U - 1, P_SWA)
            load_table(ACT.Exp)
            rows_out(U + 1, rows[:, 0, :])
            split(U + 3)
            heads_out("q0", q_t[:, 0:2, :], DH ** -0.5)
            split(U + 4)
            exps(PAIRS)
            split(U + 5)
            for pair in range(PAIRS, 2 * PAIRS):
                if pair == PAIRS + 1:
                    rows_out(U + 3, rows[:, 0, :], bank=Q1_BANKS[0])
                probs_t_out(pair)
                if pair + 1 < 2 * PAIRS:
                    exps(pair + 1)
                ot_part(pair)
                if pair == PAIRS + 1:
                    heads_out("q1", q_t[:, 4:6, :], DH ** -0.5)
                elif pair == PAIRS + 2:
                    split(U + 6)
                elif pair == 2 * PAIRS - 3:
                    split(U + 7)
                elif pair == 2 * PAIRS - 2:
                    load_table(ACT.Silu)
            split(U + 8)
            boundary(4, U_FFN3 - 1, 6)
            ffn(3)
            boundary(5, U_FFN3 + N_FFN - 1, None)

        @block.vector
        def _(dve):
            steps = [0]

            def chained(ins):
                steps[0] += 1
                ins.then_inc(dve_step, 1)
                dve.wait_ge(dve_step, steps[0])

            def split(u, i=0):
                dve.wait_ge(hi_ready, u + 1 + 3 * i)
                nc.vector.tensor_tensor(w_lo[:, u % RING], w_raw[:, u % RING], w_hi[:, u % RING].bitcast(F32),
                                        ALU.subtract).then_inc(lo_ready, 1)

            def gain(m, half):
                dve.wait_ge(gain_landed[m % GAINS], 16 * (m // GAINS + 1))
                return gains[:, m % GAINS, half * COLS:(half + 1) * COLS]

            def pregain(k, t, half):
                cols = slice(half * COLS, (half + 1) * COLS)
                nc.vector.tensor_tensor(xg[:, t, cols], x[:, t, cols], gain(PRE[k], half), ALU.mult)\
                  .then_inc(xg_ready, 1)

            def post(b, k, t):
                for half in range(2):
                    dve.wait_ge(sq_y_ready, QS * b + 2 * t + half + 1)
                    last = nc.vector.tensor_tensor(xg[:, t, half * COLS:(half + 1) * COLS],
                                                   ps[:, Y + 2 * t + half, :], gain(POST[b], half), ALU.mult)
                chained(last)
                dve.wait_ge(r_y_ready, NB * b + t + 1)
                for half in range(2):
                    cols = slice(half * COLS, (half + 1) * COLS)
                    nc.vector.scalar_tensor_tensor(out=x[:, t, cols], in0=xg[:, t, cols], scalar=r_y[:, t:t + 1],
                                                   in1=x[:, t, cols], op0=ALU.mult, op1=ALU.add).then_inc(x_ready, 1)
                    if k is not None:
                        dve.wait_ge(x_ready, QS * b + 2 * t + half + 1)
                        pregain(k, t, half)

            def xt_parts(k, t):
                for half in range(2):
                    n = 2 * t + half
                    dve.wait_ge(xt_hi_ready, QS * k + n + 1)
                    cols = (slice(None), k % 2, slice(4 * half, 4 * half + 4), slice(t * P, (t + 1) * P))
                    nc.vector.tensor_tensor(xt_lo[cols], ps[:, n, :].rearrange("p (c t) -> p c t", t=P),
                                            xt_hi[cols].bitcast(F32), ALU.subtract).then_inc(xt_ready, 1)

            def boundary(b, last_unit, k):
                post(b, k, 0)
                xt_parts(k, 0)
                split(last_unit + 2)
                post(b, k, 1)
                xt_parts(k, 1)

            def hid_step(n, i=0):
                for t in range(NB):
                    dve.wait_ge(silu_ready, NB * n + t + 1 + NB * i)
                    if n > 0 or looped(i):
                        dve.wait_ge(ht_raw, n + i)
                    nc.vector.scalar_tensor_tensor(out=hid[:, t, :], in0=ps[:, GU[t], FC:2 * FC],
                                                   scalar=r_x[:, t:t + 1], in1=silu[:, t, :], op0=ALU.mult,
                                                   op1=ALU.mult).then_inc(hid_ready, 1)

            def ht_part(n, i=0, hi=ht_hi, lo=ht_lo):
                dve.wait_ge(ht_hi_ready, n + 1 + i)
                nc.vector.tensor_tensor(lo[:, :, :], ps[:, HT, :].rearrange("p (c t) -> p c t", c=2),
                                        hi[:, :, :].bitcast(F32), ALU.subtract).then_inc(ht_ready, 1)

            def ffn(f):
                u, n = U_FFN[f], STEPS * f
                hid_step(n)
                split(u + 3)
                ht_part(n)
                split(u + 4)
                with dve.Fori(1, STEPS - 1) as i:
                    split(u + 2, i)
                    hid_step(n, i)
                    split(u + 3, i)
                    ht_part(n, i)
                    split(u + 4, i)
                split(u + 32)
                hid_step(n + STEPS - 1)
                ht_part(n + STEPS - 1, hi=ht_last_hi, lo=ht_last_lo)
                if f < 3:
                    split(u + 33)

            def rows_out(last_unit, dst, bank=ROWS[1]):
                dve.wait_ge(unit_used, last_unit + 1)
                dve.wait_ge(r_x_ready, NB * VERSION[P_FOX if last_unit < U_FFN1 else P_SWA] + NB)
                nc.vector.tensor_scalar(dst, ps[:, bank, :], r_x[:, 1:2], None, ALU.mult).then_inc(rows_dve, 1)

            def heads_out(name, dst, scale):
                dve.wait_ge(rows_t, made(TURN_ORDER, name))
                nc.vector.tensor_scalar(dst, ps[:, ROWS[1], :].rearrange("p (c t) -> p c t", c=2), scale, None,
                                        ALU.mult).then_inc(heads_dve, 1)

            def logits(pair):
                p, b, s, windowed = pair % PAIRS, pair % 2, pair % 3, pair >= PAIRS
                if not windowed:
                    dve.wait_ge(cb_raw, p + 1)
                    spread = ps[:, CB, :].rearrange("p (h s) -> p h s", h=2)
                    for cols, src in ((slice(0, P), slice(0, P)), (slice(P, SEG), slice(0, 2 * P))):
                        width = cols.stop - cols.start
                        last = nc.vector.scalar_tensor_tensor(
                            out=decay[:, :, cols], in0=spread[:, :, src], scalar=-1.0,
                            in1=causal[:, cols].unsqueeze(1).to_broadcast([P, 2, width]), op0=ALU.mult, op1=ALU.add)
                    last.then_inc(decay_ready, 1)
                    dve.wait_ge(decay_ready, p + 1)
                dve.wait_ge(sc_raw, pair + 1)
                if pair >= 3:
                    dve.wait_ge(pt_raw, pair - 2)
                for j in range(2):
                    h = 2 * p + j
                    if windowed:
                        slope = float(np.float32(2.0) ** np.float32(-8.0 * (h + 1) / H))
                        last = nc.vector.scalar_tensor_tensor(out=probs[:, s, j, :], in0=dist, scalar=-slope,
                                                              in1=ps[:, SC[j], 0:SEG], op0=ALU.mult, op1=ALU.add)
                    else:
                        for t, cols in enumerate((slice(0, P), slice(P, SEG))):
                            last = nc.vector.scalar_tensor_tensor(
                                out=probs[:, s, j, cols], in0=ps[:, SC[j], cols], scalar=c_tok[:, t, h:h + 1],
                                in1=decay[:, j, cols], op0=ALU.add, op1=ALU.add)
                last.then_inc(logits_done, 1)
                dve.wait_ge(logits_done, pair + 1)
                nc.vector.reduce_max(mx[:, b, :, 0], probs[:, s, :, 0:P], AX.X)
                chained(nc.vector.reduce_max(mx[:, b, :, 1], probs[:, s, :, P:SEG], AX.X))
                if windowed:
                    sink = sinks[:, 2 * p:2 * p + 2].unsqueeze(2).to_broadcast([P, 2, NB])
                    chained(nc.vector.tensor_tensor(mx[:, b], mx[:, b], sink, ALU.max))
                    nc.vector.tensor_tensor(sink_d[:, b], sink, mx[:, b], ALU.subtract)
                nc.vector.tensor_scalar(neg_mx[:, b], mx[:, b], -1.0, None, ALU.mult).then_inc(neg_mx_ready, 1)

            def normalise(pair):
                b, s = pair % 2, pair % 3
                dve.wait_ge(exp_ready, pair + 1)
                if pair >= PAIRS:
                    chained(nc.vector.tensor_tensor(sums[:, b], sums[:, b], sink_e[:, b], ALU.add))
                chained(nc.vector.reciprocal(recip[:, b], sums[:, b]))
                for j in range(2):
                    for t, cols in enumerate((slice(0, P), slice(P, SEG))):
                        last = nc.vector.tensor_scalar(probs[:, s, j, cols], probs[:, s, j, cols],
                                                       recip[:, b, j, t:t + 1], None, ALU.mult)
                last.then_inc(probs_ready, 1)

            def ot_part(pair):
                dve.wait_ge(ot_hi_ready, pair + 1)
                nc.vector.tensor_tensor(xt_lo[:, 0, pair % PAIRS, :], ps[:, ot_bank(pair), 0:NB * P],
                                        xt_hi[:, 0, pair % PAIRS, :].bitcast(F32), ALU.subtract).then_inc(ot_ready, 1)

            def qk_rows_out(g):
                rows_out(U_FOX + QK[g] + 1, rows[:, 1, :])

            def k_out(g):
                heads_out(f"qk{g}", k_t[:, 2 * g:2 * g + 2, :], 1.0)

            for t in range(NB):
                dve.wait_ge(x_landed[t], 16)
                for half in range(2):
                    pregain(0, t, half)
            for t in range(NB):
                xt_parts(0, t)
            split(0)
            split(1)
            split(2)
            ffn(0)

            U = U_FOX
            dve.wait_ge(wf_hi_ready, 1)
            dve.wait_ge(table_landed, 16)
            nc.vector.tensor_tensor(wf_lo[:, :, 0:H], wf_raw[:, :, :], wf_hi[:, :, 0:H].bitcast(F32),
                                    ALU.subtract).then_inc(wf_ready, 1)
            boundary(0, U - 1, P_FOX)
            split(U + 2)
            qk_rows_out(0)
            split(U + 3)
            k_out(0)
            dve.wait_ge(f_t_raw, 1)
            f_tok = ps[:, 1, 0:NB * H].rearrange("p (t h) -> p t h", h=H)
            for t in range(NB):
                last = nc.vector.scalar_tensor_tensor(out=fz[:, 0, t, :], in0=f_tok[:, t, :], scalar=r_x[:, t:t + 1],
                                                      in1=bf[:, :], op0=ALU.mult, op1=ALU.add)
            chained(last)
            chained(nc.vector.scalar_tensor_tensor(out=fz[:, 1], in0=fz[:, 0], scalar=-1.0, in1=fz[:, 0],
                                                   op0=ALU.mult, op1=ALU.min))
            nc.vector.tensor_scalar(fz[:, 0], fz[:, 0], 0.0, None, ALU.min).then_inc(fz_ready, 1)
            split(U + 4)
            dve.wait_ge(fe_ready, 1)
            nc.vector.tensor_tensor(logf[:, :, :], fz[:, 0], fz[:, 3], ALU.subtract).then_inc(logf_ready, 1)
            split(U + 5)
            rows_out(U + V[0] + 1, v_rows[:, 1, 0:COLS], bank=V0_BANKS[1])
            logits(0)
            split(U + 6)
            normalise(0)
            logits(1)
            split(U + 7)
            normalise(1)
            qk_rows_out(1)
            ot_part(0)
            k_out(1)
            logits(2)
            split(U + 8)
            normalise(2)
            ot_part(1)
            logits(3)
            split(U + 9)
            normalise(3)
            qk_rows_out(2)
            ot_part(2)
            k_out(2)
            logits(4)
            split(U + 10)
            normalise(4)
            ot_part(3)
            split(U + 11)
            rows_out(U + V[1] + 1, v_rows[:, 1, COLS:D])
            logits(5)
            split(U + 12)
            normalise(5)
            ot_part(4)
            split(U + 13)
            qk_rows_out(3)
            ot_part(5)
            k_out(3)
            logits(6)
            normalise(6)
            logits(7)
            split(U + 14)
            normalise(7)
            ot_part(6)
            split(U + 15)
            ot_part(7)
            split(U + 16)
            boundary(1, U_FFN1 - 1, 2)
            split(U_FFN1 + 2)
            ffn(1)

            boundary(2, U_KV - 1, P_KV)
            for half in range(2):
                dve.wait_ge(xt_raw, QS * P_KV + 2)
                pregain(4, 0, half)
            split(U_FFN2)
            xt_parts(4, 0)
            for half in range(2):
                dve.wait_ge(xt_raw, QS * P_KV + 4)
                pregain(4, 1, half)
            split(U_FFN2 + 1)
            dve.wait_ge(unit_used, U_KV + 2)
            dve.wait_ge(r_x_ready, NB * VERSION[P_KV] + NB)
            for twin in range(2):
                nc.vector.tensor_scalar(rows[:, 1, :].rearrange("p (h s d) -> p h s d", s=2, d=DH)[:, :, twin, :],
                                        ps[:, ROWS[1], 0:KVH * DH].rearrange("p (h d) -> p h d", d=DH), r_x[:, 1:2],
                                        None, ALU.mult)
            nc.vector.tensor_scalar(v_rows[:, 1, 0:KVH * DH], ps[:, ROWS[1], KVH * DH:COLS], r_x[:, 1:2], None,
                                    ALU.mult).then_inc(rows_dve, 1)
            xt_parts(4, 1)
            split(U_FFN2 + 2)
            heads_out("kv", k_t[:, 2:4, :], 1.0)
            ffn(2)

            U = U_SWA
            boundary(3, U - 1, P_SWA)
            split(U + 2)
            rows_out(U + 1, rows[:, 1, :])
            heads_out("q0", q_t[:, 2:4, :], DH ** -0.5)
            logits(PAIRS)
            split(U + 3)
            normalise(PAIRS)
            logits(PAIRS + 1)
            for pair in range(PAIRS, 2 * PAIRS):
                if pair == PAIRS + 1:
                    rows_out(U + 3, rows[:, 1, :], bank=Q1_BANKS[1])
                if pair + 2 < 2 * PAIRS:
                    logits(pair + 2)
                if pair + 1 < 2 * PAIRS:
                    normalise(pair + 1)
                ot_part(pair)
                if pair == PAIRS + 1:
                    heads_out("q1", q_t[:, 6:8, :], DH ** -0.5)
                    split(U + 4)
                elif pair == PAIRS + 2:
                    split(U + 5)
                elif pair == PAIRS + 3:
                    split(U + 6)
                elif pair == 2 * PAIRS - 2:
                    split(U + 7)
            split(U + 8)
            boundary(4, U_FFN3 - 1, 6)
            split(U_FFN3 + 2)
            ffn(3)
            post(5, None, 0)
            post(5, None, 1)

        @block.tensor
        def _(pe):
            def transpose_x(k, t):
                for half in range(2):
                    pe.wait_ge(xg_ready, QS * k + 2 * t + half + 1)
                    for c in range(4):
                        last = nc.tensor.transpose(ps[:, 2 * t + half, c * P:(c + 1) * P],
                                                   xg[:, t, (4 * half + c) * P:(4 * half + c + 1) * P], ident)
                    last.then_inc(xt_raw, 1)

            def half_unit(u, t, parity, half, bank, chunks=range(4)):
                slot = u % RING
                for k in chunks:
                    left = (slice(None), parity, 4 * half + k, slice(t * P, (t + 1) * P))
                    start, stop = half == 0 and k == 0, half == 1 and k == 3
                    nc.tensor.matmul(ps[:, bank, :], xt_hi[left], w_hi[:, slot, k, :], start=start, stop=False)
                    nc.tensor.matmul(ps[:, bank, :], xt_hi[left], w_lo[:, slot, k, :], start=False, stop=False)
                    last = nc.tensor.matmul(ps[:, bank, :], xt_lo[left], w_hi[:, slot, k, :], start=False, stop=stop)
                return last

            def unit(u, parity, half, banks, block0_done=None, i=0):
                pe.wait_ge(lo_ready, u + 1 + 3 * i)
                last = half_unit(u, 0, parity, half, banks[0])
                if block0_done is not None:
                    last.then_inc(block0_done, 1)
                half_unit(u, 1, parity, half, banks[1]).then_inc(unit_used, 1)

            def first_units(k, u, parity, banks, block0_done=None):
                for t in range(NB):
                    if k > 0:
                        transpose_x(k, t)
                    elif t == 0:
                        transpose_x(k, 0)
                        transpose_x(k, 1)
                    for half in range(2):
                        pe.wait_ge(xt_ready, QS * k + 2 * t + half + 1)
                        pe.wait_ge(lo_ready, u + half + 1)
                        last = half_unit(u + half, t, parity, half, banks[t])
                        if t == 1:
                            last.then_inc(unit_used, 1)
                    if t == 0 and block0_done is not None:
                        last.then_inc(block0_done, 1)

            def keys_values_and_first_units(u):
                k = P_KV
                transpose_x(k, 0)
                for half in range(2):
                    pe.wait_ge(xt_ready, QS * k + half + 1)
                    pe.wait_ge(lo_ready, U_KV + half + 1)
                    half_unit(U_KV + half, 0, 1, half, ROWS[0])
                transpose_x(k, 1)
                pe.wait_ge(xt_ready, QS * k + 3)
                half_unit(U_KV, 1, 1, 0, ROWS[1]).then_inc(unit_used, 1)
                transpose_x(k + 1, 0)
                pe.wait_ge(xt_ready, QS * k + 4)
                half_unit(U_KV + 1, 1, 1, 1, ROWS[1]).then_inc(unit_used, 1)
                pe.wait_ge(xt_ready, QS * (k + 1) + 1)
                pe.wait_ge(lo_ready, u + 1)
                half_unit(u, 0, 0, 0, GU[0])
                pe.wait_ge(xt_ready, QS * (k + 1) + 2)
                pe.wait_ge(lo_ready, u + 2)
                half_unit(u + 1, 0, 0, 1, GU[0], range(2))
                transpose_x(k + 1, 1)
                half_unit(u + 1, 0, 0, 1, GU[0], range(2, 4)).then_inc(gu0_ready, 1)
                for half in range(2):
                    pe.wait_ge(xt_ready, QS * (k + 1) + half + 3)
                    half_unit(u + half, 1, 0, half, GU[1]).then_inc(unit_used, 1)
                turn("kv")
                heads_done("kv")

            def clear_y():
                for bank in range(Y, Y + 4):
                    nc.tensor.matmul(ps[:, bank, :], zeros[:, 0:P], zeros[:, :], start=True, stop=False,
                                     skip_group_check=True)

            def transpose_h(n, i=0):
                for t in range(NB):
                    pe.wait_ge(hid_ready, NB * n + t + 1 + NB * i)
                    for c in range(2):
                        last = nc.tensor.transpose(ps[:, HT, (2 * c + t) * P:(2 * c + t + 1) * P],
                                                   hid[:, t, c * P:(c + 1) * P], ident)
                last.then_inc(ht_raw, 1)

            def down_part(u, t, c, hi=ht_hi, lo=ht_lo, stop=False):
                slot, tokens = u % RING, slice(t * P, (t + 1) * P)
                for left, w in ((hi, w_hi), (hi, w_lo), (lo, w_hi)):
                    for half in range(2):
                        last = nc.tensor.matmul(ps[:, Y + 2 * t + half, :], left[:, c, tokens],
                                                w[:, slot, 2 * c + half, :], start=False,
                                                stop=stop and left is lo, skip_group_check=True)
                return last

            def down(u, n, i=0):
                pe.wait_ge(ht_ready, n + 1 + i)
                pe.wait_ge(lo_ready, u + 1 + 3 * i)
                for t in range(NB):
                    for c in range(2):
                        last = down_part(u, t, c)
                last.then_inc(unit_used, 1)

            def ffn(f):
                u, n, k = U_FFN[f], STEPS * f, FFN_PREP[f]
                if k == P_KV + 1:
                    keys_values_and_first_units(u)
                else:
                    first_units(k, u, 0, GU, block0_done=gu0_ready)
                clear_y()
                with pe.Fori(0, STEPS - 2) as i:
                    transpose_h(n, i)
                    unit(u + 2, 0, 0, GU, i=i)
                    unit(u + 3, 0, 1, GU, block0_done=gu0_ready, i=i)
                    down(u + 4, n, i=i)
                n += STEPS - 2
                transpose_h(n)
                unit(u + 29, 0, 0, GU)
                unit(u + 30, 0, 1, GU, block0_done=gu0_ready)
                pe.wait_ge(ht_ready, n + 1)
                pe.wait_ge(lo_ready, u + 32)
                down_part(u + 31, 0, 0)
                down_part(u + 31, 0, 1)
                transpose_h(n + 1)
                down_part(u + 31, 1, 0)
                pe.wait_ge(ht_ready, n + 2)
                pe.wait_ge(lo_ready, u + 33)
                down_part(u + 32, 0, 0, ht_last_hi, ht_last_lo)
                down_part(u + 32, 0, 1, ht_last_hi, ht_last_lo, stop=True).then_inc(y0_ready, 1)
                down_part(u + 31, 1, 1).then_inc(unit_used, 1)
                down_part(u + 32, 1, 0, ht_last_hi, ht_last_lo)
                down_part(u + 32, 1, 1, ht_last_hi, ht_last_lo, stop=True).then_inc(unit_used, 1)

            def rows_done(name):
                pe.wait_ge(rows_act, made(ROW_ORDER, name))
                pe.wait_ge(rows_dve, made(ROW_ORDER, name))

            def heads_done(name):
                pe.wait_ge(heads_act, made(TURN_ORDER, name))
                pe.wait_ge(heads_dve, made(TURN_ORDER, name))

            def turn(name):
                rows_done(name)
                for c in range(4):
                    for t in range(NB):
                        at = ((c % 2) * 2 + t) * P
                        last = nc.tensor.transpose(ps[:, ROWS[c // 2], at:at + P], rows[:, t, c * P:(c + 1) * P],
                                                   ident)
                last.then_inc(rows_t, 1)

            def forget_gates():
                pe.wait_ge(wf_ready, 1)
                for c in range(DC):
                    for left, right in ((wf_hi, xt_hi), (wf_hi, xt_lo), (wf_lo, xt_hi)):
                        last = nc.tensor.matmul(ps[:, 0, 0:NB * P], left[:, c, :], right[:, P_FOX % 2, c, :],
                                                start=c == 0 and left is wf_hi and right is xt_hi,
                                                stop=c == DC - 1 and left is wf_lo)
                last.then_inc(f_raw, 1)

            def forget_tokens():
                pe.wait_ge(f_rows_ready, 1)
                for t in range(NB):
                    last = nc.tensor.transpose(ps[:, 1, t * H:(t + 1) * H], f_rows[:, t * P:(t + 1) * P],
                                               ident[0:H, 0:H])
                last.then_inc(f_t_raw, 1)

            def forget_sums():
                pe.wait_ge(logf_ready, 1)
                nc.tensor.matmul(ps[0:H, 1, 0:NB * P], logf[:, 0, :], tri_ones, start=True, stop=False)
                nc.tensor.matmul(ps[0:H, 1, P:NB * P], logf[:, 1, :], tri, start=False, stop=True)
                c = ps[:, 1, NB * P:NB * P + NB * H]
                nc.tensor.matmul(c[:, 0:H], tri, logf[:, 0, :], start=True, stop=True)
                nc.tensor.matmul(c[:, H:2 * H], ones, logf[:, 0, :], start=True, stop=False)
                nc.tensor.matmul(c[:, H:2 * H], tri, logf[:, 1, :], start=False, stop=True).then_inc(c_raw, 1)

            def scores(pair):
                p, windowed = pair % PAIRS, pair >= PAIRS
                if not windowed:
                    if p:
                        pe.wait_ge(decay_ready, p)
                    for j in range(2):
                        h = 2 * p + j
                        last = nc.tensor.matmul(ps[:, CB, j * NB * P:(j + 1) * NB * P],
                                                ident[0:H, h:h + 1].to_broadcast([H, P]), c_t[:, :], start=True,
                                                stop=True)
                    last.then_inc(cb_raw, 1)
                if pair == PAIRS + 4:
                    heads_done("q1")
                if pair:
                    pe.wait_ge(logits_done, pair)
                for j in range(2):
                    heads = slice(j * DH, (j + 1) * DH)
                    keys = k_t[heads, p // 2 if windowed else p, :]
                    nc.tensor.matmul(ps[:, SC[j], 0:P], q_t[heads, p, 0:P], keys[:, 0:P], start=True, stop=True)
                    last = nc.tensor.matmul(ps[:, SC[j], P:SEG], q_t[heads, p, P:NB * P], keys, start=True, stop=True)
                last.then_inc(sc_raw, 1)

            def transpose_probs(pair):
                pe.wait_ge(probs_ready, pair + 1)
                if pair:
                    pe.wait_ge(pt_ready, pair)
                for j in range(2):
                    for n in range(3):
                        last = nc.tensor.transpose(ps[:, PTB[j], n * P:(n + 1) * P],
                                                   probs[:, pair % 3, j, n * P:(n + 1) * P], ident)
                last.then_inc(pt_raw, 1)

            def values(pair):
                p = pair % PAIRS
                pe.wait_ge(pt_ready, pair + 1)
                if pair:
                    pe.wait_ge(ot_ready, pair)
                if ot_bank(pair) != OT:
                    pe.wait_ge(logits_done, pair - p + PAIRS)
                for j in range(2):
                    h = (2 * p + j) // 4 if pair >= PAIRS else 2 * p + j
                    v = v_rows[:, :, h * DH:(h + 1) * DH]
                    o = ps[j * DH:(j + 1) * DH, ot_bank(pair), 0:NB * P]
                    pt = probs_t[:, pair % 2, j, :]
                    nc.tensor.matmul(o, v[:, 0, :], pt[:, 0:2 * P], start=True, stop=False)
                    last = nc.tensor.matmul(o[:, P:2 * P], v[:, 1, :], pt[:, 2 * P:SEG], start=False, stop=True)
                last.then_inc(ot_raw, 1)

            def out_part(u, n, t, pairs_done, chunks=range(4)):
                pe.wait_ge(lo_ready, u + n + 1)
                last = PAIRS - 2 if n == 1 and t == 0 else 4 * (n // 2) + chunks[-1] + 1
                pe.wait_ge(ot_ready, pairs_done + last)
                return half_unit(u + n, t, 0, n // 2, Y + 2 * t + 1 - n % 2, chunks)

            def output_rest(u, pairs_done, done=0):
                out_part(u, 2, 0, pairs_done, range(done, 3))
                values(pairs_done + PAIRS - 1)
                out_part(u, 3, 0, pairs_done, range(3))
                out_part(u, 2, 0, pairs_done, range(3, 4))
                out_part(u, 3, 0, pairs_done, range(3, 4)).then_inc(y0_ready, 1)
                out_part(u, 2, 1, pairs_done, range(done, 4)).then_inc(unit_used, 1)
                out_part(u, 3, 1, pairs_done).then_inc(unit_used, 1)

            pe.wait_ge(ident_landed, 16)
            pe.wait_ge(zeros_ready, 3)
            ffn(0)
            pe.wait_ge(table_landed, 16)

            U = U_FOX
            first_units(P_FOX, U + QK[0], 1, ROWS)
            forget_gates()
            turn("qk0")
            forget_tokens()
            unit(U + V[0], 1, 0, V0_BANKS)
            forget_sums()
            unit(U + V[0] + 1, 1, 1, V0_BANKS)
            pe.wait_ge(c_ready, 1)
            heads_done("qk0")
            scores(0)
            unit(U + QK[1], 1, 0, ROWS)
            scores(1)
            rows_done("v0")
            transpose_probs(0)
            unit(U + QK[1] + 1, 1, 1, ROWS)
            values(0)
            turn("qk1")
            transpose_probs(1)
            heads_done("qk1")
            scores(2)
            unit(U + QK[2], 1, 0, ROWS)
            values(1)
            scores(3)
            transpose_probs(2)
            unit(U + QK[2] + 1, 1, 1, ROWS)
            values(2)
            turn("qk2")
            transpose_probs(3)
            heads_done("qk2")
            scores(4)
            unit(U + V[1], 1, 0, ROWS)
            values(3)
            transpose_probs(4)
            unit(U + V[1] + 1, 1, 1, ROWS)
            scores(5)
            rows_done("v1")
            unit(U + QK[3], 1, 0, ROWS)
            values(4)
            transpose_probs(5)
            unit(U + QK[3] + 1, 1, 1, ROWS)
            values(5)
            turn("qk3")
            out_part(U + F_OUT, 1, 0, 0)
            heads_done("qk3")
            scores(6)
            out_part(U + F_OUT, 0, 0, 0)
            scores(7)
            out_part(U + F_OUT, 0, 1, 0).then_inc(unit_used, 1)
            transpose_probs(6)
            pe.wait_ge(decay_ready, PAIRS)
            out_part(U + F_OUT, 1, 1, 0).then_inc(unit_used, 1)
            values(6)
            transpose_probs(7)
            output_rest(U + F_OUT, 0)
            ffn(1)

            ffn(2)

            U = U_SWA
            first_units(P_SWA, U, 1, ROWS)
            pe.wait_ge(lo_ready, U + 3)
            half_unit(U + 2, 0, 1, 0, Q1_BANKS[0])
            turn("q0")
            heads_done("q0")
            scores(PAIRS)
            half_unit(U + 2, 1, 1, 0, Q1_BANKS[1]).then_inc(unit_used, 1)
            scores(PAIRS + 1)
            pe.wait_ge(lo_ready, U + 4)
            half_unit(U + 3, 0, 1, 1, Q1_BANKS[0])
            out = U + S_OUT
            for pair in range(PAIRS, 2 * PAIRS):
                transpose_probs(pair)
                if pair + 2 < 2 * PAIRS:
                    scores(pair + 2)
                if pair == 2 * PAIRS - 1:
                    break
                if pair == 2 * PAIRS - 2:
                    out_part(out, 1, 0, PAIRS).then_inc(unit_used, 1)
                values(pair)
                if pair == PAIRS:
                    half_unit(U + 3, 1, 1, 1, Q1_BANKS[1]).then_inc(unit_used, 1)
                elif pair == PAIRS + 1:
                    turn("q1")
                elif pair == PAIRS + 2:
                    out_part(out, 0, 0, PAIRS, range(0, 2))
                    out_part(out, 0, 1, PAIRS, range(0, 2))
                elif pair == PAIRS + 3:
                    out_part(out, 0, 0, PAIRS, range(2, 3))
                    out_part(out, 0, 1, PAIRS, range(2, 3))
                    out_part(out, 1, 1, PAIRS, range(0, 2))
                elif pair == PAIRS + 4:
                    out_part(out, 0, 0, PAIRS, range(3, 4))
                    out_part(out, 0, 1, PAIRS, range(3, 4)).then_inc(unit_used, 1)
                    out_part(out, 1, 1, PAIRS, range(2, 4))
                elif pair == PAIRS + 5:
                    out_part(out, 2, 0, PAIRS, range(0, 1))
                    out_part(out, 2, 1, PAIRS, range(0, 1))
            output_rest(out, PAIRS, done=1)
            ffn(3)


_INS = ["x", "ffn_w_gate", "ffn_w_up", "ffn_w_down", "norm_g", "a_w_in", "a_b_f", "a_w_o", "kv_norm_g", "b_w_kv",
        "b_w_q", "b_sinks", "b_w_o"]
_OUTS = [((1, NB * P, D), "float32")]


def kernel(**inputs):
    import numpy as _np
    import concourse.bacc as _bacc
    from concourse import mybir as _mybir
    from concourse.bass_utils import run_bass_kernel_spmd as _run

    nc = _bacc.Bacc("TRN2", target_bir_lowering=False, num_devices=1)
    arrays, args = {}, []
    for name in [*_INS, "tables"]:
        a = _np.ascontiguousarray(constants() if name == "tables" else inputs[name])
        arrays[f"in_{name}_dram"] = a
        args.append(nc.dram_tensor(f"in_{name}_dram", a.shape, _mybir.dt.from_np(a.dtype), kind="ExternalInput").ap())
    for i, (shape, dtype) in enumerate(_OUTS):
        dt = _mybir.dt.from_np(_np.dtype(dtype))
        args.append(nc.dram_tensor(f"out_{i}_dram", shape, dt, kind="ExternalOutput").ap())
    trunk(nc, *args)
    r = _run(nc, [arrays], core_ids=[0])
    return r.results[0]["out_0_dram"]
```

```python
from contextlib import ExitStack

import numpy as np

import concourse.bass as bass
from concourse import mybir

F32 = mybir.dt.float32
F32R = mybir.dt.float32r
ALU = mybir.AluOpType
ACT = mybir.ActivationFunctionType
AX = mybir.AxisListType

P = 128
NB = 2
D = 1024
DC = D // P
F = 2816
FC = 256
STEPS = F // FC
DH = 64
H = D // DH
PAIRS = H // 2
KVH = 4
COLS = 512
RING = 3
DMAS = 2
EPS = 1e-6
SEG = 3 * P
MASKED = -1.0e38
FAR = 1.0e38
GAINS = 3

GU = (0, 1)
HT = 2
Y = 4
SC = (0, 1)
PTB = (2, 3)
OT = 4
CB = 6
V0_BANKS = (2, 3)
FIRST_ROWS = (5, 6)
Q1_BANKS = (7, 6)
ROWS = (5, 7)


def constants():
    k, s = np.arange(P)[:, None], np.arange(P)[None, :]
    ident = np.eye(P)
    tri = k <= s
    diag = np.where(s <= k, 0.0, MASKED)
    causal = np.concatenate([diag, np.zeros((P, P)), diag], 1)
    q0, q1, keys = k, k + P, np.arange(2 * P)[None, :]

    def band(q, key):
        near = (key // 64 <= q // 64) & (key // 64 >= q // 64 - 1)
        return np.where(near, np.abs(q - key), FAR)

    dist = np.concatenate([band(q0, keys[:, :P]), band(q1, keys)], 1)
    return np.concatenate([ident, tri, np.ones((P, P)), causal, dist], 1).astype(np.float32)


def trunk(nc, x_in, w_gate, w_up, w_down, norm_g, a_w_in, a_b_f, a_w_o, kv_norm_g, b_w_kv, b_w_q,
          b_sinks, b_w_o, tables, out):
    ctx = ExitStack()
    with ctx:
        def sb(name, shape, dt=F32):
            return ctx.enter_context(nc.sbuf_tensor(name, shape, dt))

        def sem(name):
            return ctx.enter_context(nc.semaphore(name))

        w_raw = sb("w_raw", [P, RING, 4, COLS])
        w_hi = sb("w_hi", [P, RING, 4, COLS], F32R)
        w_lo = sb("w_lo", [P, RING, 4, COLS], F32R)
        x = sb("x", [P, NB, D])
        xg = sb("xg", [P, NB, D])
        squares = sb("squares", [P, D], mybir.dt.bfloat16)
        gains = sb("gains", [P, GAINS, D])
        xt_hi = sb("xt_hi", [P, 2, DC, NB * P], F32R)
        xt_lo = sb("xt_lo", [P, 2, DC, NB * P], F32R)
        ht_hi = sb("ht_hi", [P, 2, NB * P], F32R)
        ht_lo = sb("ht_lo", [P, 2, NB * P], F32R)
        ht_last_hi = sb("ht_last_hi", [P, 2, NB * P], F32R)
        ht_last_lo = sb("ht_last_lo", [P, 2, NB * P], F32R)
        zeros = sb("zeros", [P, COLS], F32R)
        rows = sb("rows", [P, NB, COLS])
        silu = rows[:, 0, :].rearrange("p (t f) -> p t f", t=NB)
        hid = rows[:, 1, :].rearrange("p (t f) -> p t f", t=NB)
        v_rows = sb("v_rows", [P, NB, D])
        q_t = sb("q_t", [P, PAIRS, NB * P])
        k_t = sb("k_t", [P, PAIRS, NB * P])
        probs = sb("probs", [P, 3, 2, SEG])
        probs_t = sb("probs_t", [P, 2, 2, SEG])
        decay = sb("decay", [P, 2, SEG])
        table = sb("table", [P, 3 * P + 2 * SEG])
        ident, tri, ones = table[:, 0:P], table[:, P:2 * P], table[:, 2 * P:3 * P]
        tri_ones = table[:, P:3 * P]
        causal, dist = table[:, 3 * P:3 * P + SEG], table[:, 3 * P + SEG:]
        wf_raw = sb("wf_raw", [P, DC, H])
        wf_hi = sb("wf_hi", [P, DC, P], F32R)
        wf_lo = sb("wf_lo", [P, DC, P], F32R)
        f_rows = sb("f_rows", [H, NB * P])
        fz = sb("fz", [P, 4, NB, H])
        logf = sb("logf", [P, NB, H])
        c_tok = sb("c_tok", [P, NB, H])
        c_hi = sb("c_hi", [H, NB * P], F32R)
        c_lo = sb("c_lo", [H, NB * P], F32R)
        pick = sb("pick", [H, H], F32R)
        bf = sb("bf", [P, H])
        sinks = sb("sinks", [P, H])
        half_power = sb("half_power", [P, 1])
        unread = sb("unread", [P, 8])
        ss_y = sb("ss_y", [P, NB, 2])
        ss_x = sb("ss_x", [P, NB])
        r_y = sb("r_y", [P, NB])
        r_x = sb("r_x", [P, NB])
        r_tmp = sb("r_tmp", [P, 2, NB])
        mx = sb("mx", [P, 2, 2, NB])
        neg_mx = sb("neg_mx", [P, 2, 2, NB])
        sums = sb("sums", [P, 2, 2, NB])
        sink_d = sb("sink_d", [P, 2, 2, NB])
        sink_e = sb("sink_e", [P, 2, 2, NB])
        recip = sb("recip", [P, 2, 2, NB])
        ps = ctx.enter_context(nc.psum_tensor("ps", [P, 8, 512], F32))

        raw_landed = [sem(f"raw_landed{i}") for i in range(RING)]
        hi_ready, lo_ready, unit_used = sem("hi_ready"), sem("lo_ready"), sem("unit_used")
        hi_half_ready, lo_half_ready = sem("hi_half_ready"), sem("lo_half_ready")
        x_landed = [sem(f"x_landed{t}") for t in range(NB)]
        gain_landed = [sem(f"gain_landed{i}") for i in range(GAINS)]
        ident_landed, table_landed, small_landed = sem("ident_landed"), sem("table_landed"), sem("small_landed")
        out_done = sem("out_done")
        zeros_ready, wf_hi_ready, wf_ready = sem("zeros_ready"), sem("wf_hi_ready"), sem("wf_ready")
        pool_step, dve_step, act_step = sem("pool_step"), sem("dve_step"), sem("act_step")
        sq_y_ready, r_y_ready, sq_x_ready, r_x_ready = (sem("sq_y_ready"), sem("r_y_ready"), sem("sq_x_ready"),
                                                        sem("r_x_ready"))
        x_ready, xg_ready, xt_raw = sem("x_ready"), sem("xg_ready"), sem("xt_raw")
        xt_hi_ready, xt_ready = sem("xt_hi_ready"), sem("xt_ready")
        gu0_ready, silu_ready, hid_ready, ht_raw = (sem("gu0_ready"), sem("silu_ready"), sem("hid_ready"),
                                                    sem("ht_raw"))
        ht_hi_ready, ht_ready, y0_ready = sem("ht_hi_ready"), sem("ht_ready"), sem("y0_ready")
        c_lo_ready = sem("c_lo_ready")
        f_raw, f_rows_ready, f_t_raw, fz_ready, fe_ready = (sem("f_raw"), sem("f_rows_ready"), sem("f_t_raw"),
                                                            sem("fz_ready"), sem("fe_ready"))
        logf_ready, c_raw, c_ready = sem("logf_ready"), sem("c_raw"), sem("c_ready")
        rows_act, rows_dve, rows_t = sem("rows_act"), sem("rows_dve"), sem("rows_t")
        heads_act, heads_dve = sem("heads_act"), sem("heads_dve")
        cb_raw, decay_ready, sc_raw, logits_done = (sem("cb_raw"), sem("decay_ready"), sem("sc_raw"),
                                                    sem("logits_done"))
        neg_mx_ready, exp_ready, probs_ready = sem("neg_mx_ready"), sem("exp_ready"), sem("probs_ready")
        pt_raw, pt_ready, ot_raw, ot_hi_ready, ot_ready = (sem("pt_raw"), sem("pt_ready"), sem("ot_raw"),
                                                           sem("ot_hi_ready"), sem("ot_ready"))

        N_FFN, N_FOX, N_KV, N_SWA = 3 * STEPS, 16, 2, 8
        U_FFN0 = 0
        U_FOX = U_FFN0 + N_FFN
        U_FFN1 = U_FOX + N_FOX
        U_KV = U_FFN1 + N_FFN
        U_FFN2 = U_KV + N_KV
        U_SWA = U_FFN2 + N_FFN
        U_FFN3 = U_SWA + N_SWA
        U_FFN = [U_FFN0, U_FFN1, U_FFN2, U_FFN3]
        QK = [0, 4, 6, 10]
        V = [2, 8]
        F_OUT, S_OUT = 12, 4
        ROW_ORDER = ["qk0", "v0", "qk1", "qk2", "v1", "qk3", "kv", "q0", "q1"]
        TURN_ORDER = ["qk0", "qk1", "qk2", "qk3", "kv", "q0", "q1"]

        FFN_PREP = [0, 2, 4, 6]
        P_FOX, P_KV, P_SWA = 1, 3, 5
        VERSION = [0, 1, 2, 3, 3, 4, 5]
        GAIN_ROWS = [(0, 0), (0, 1), (0, 2), (0, 3), (0, 4), (0, 5), None, (1, 0), (1, 1), (1, 2), (1, 3), (1, 4),
                     (1, 5)]
        PRE = [0, 2, 4, 6, 7, 9, 11]
        POST = [1, 3, 5, 8, 10, 12]
        BOUNDARY = {1: 0, 2: 1, 3: 2, 5: 3, 6: 4}
        SUBLAYERS = len(POST)
        WEIGHT = [4.0, 1.0, 4.0, 4.0, 1.0, 4.0]
        QS = 2 * NB

        def made(order, name):
            return order.index(name) + 1

        def ot_bank(pair):
            last = pair % PAIRS - (PAIRS - 2)
            return OT if last < 0 else SC[last]

        def turn_banks(name):
            return PTB if name == "q0" else ROWS

        def looped(i):
            return not isinstance(i, int)

        block = ctx.enter_context(nc.Block())

        @block.sync
        def _(sp):
            def load_gain(m):
                before = m - GAINS
                if before >= 0 and before in PRE:
                    sp.wait_ge(xg_ready, QS * (PRE.index(before) + 1))
                elif before >= 0:
                    sp.wait_ge(x_ready, QS * (POST.index(before) + 1))
                row = GAIN_ROWS[m]
                src = kv_norm_g if row is None else norm_g[row[0], row[1]]
                sp.dma_start(gains[:, m % GAINS, :], src.partition_broadcast(P)).then_inc(gain_landed[m % GAINS], 16)

            def load(u, pieces, i=0):
                if u >= RING or looped(i):
                    sp.wait_ge(lo_ready, u - RING + 1 + 3 * i)
                for dst, src in pieces:
                    sp.dma_start(dst, src).then_inc(raw_landed[u % RING], 16)

            def columns(u, w, cols, half):
                width = COLS // len(cols)
                load(u, [(w_raw[:, u % RING, :, n * width:(n + 1) * width],
                          w[half * 4 * P:(half + 1) * 4 * P, col:col + width].rearrange("(k p) n -> p k n", p=P))
                         for n, col in enumerate(cols)])

            def gate_up(u, l, j, half, step, i=0):
                rws = slice(half * 4 * P, (half + 1) * 4 * P)
                cols = bass.ds(step * FC, FC)
                load(u, [(w_raw[:, u % RING, :, n * FC:(n + 1) * FC],
                          w[l, j, rws, cols].rearrange("(k p) f -> p k f", p=P))
                         for n, w in enumerate((w_gate, w_up))], i)

            def down(u, l, j, step, i=0):
                load(u, [(w_raw[:, u % RING, 2 * n:2 * n + 2, :].rearrange("p a b -> p (a b)"),
                          w_down[l, j, bass.ds(step * FC + n * P, P), :]) for n in range(2)], i)

            def load_x(t):
                sp.dma_start(x[:, t, :], x_in[0, t * P:(t + 1) * P, :]).then_inc(x_landed[t], 16)

            def ffn(f, next_gains):
                l, j, u = f // 2, f % 2, U_FFN[f]
                gate_up(u, l, j, 0, 0)
                if f == 0:
                    load_x(1)
                gate_up(u + 1, l, j, 1, 0)
                gate_up(u + 2, l, j, 0, 1)
                gate_up(u + 3, l, j, 1, 1)
                down(u + 4, l, j, 0)
                for m in next_gains:
                    load_gain(m)
                with sp.Fori(1, STEPS - 1) as i:
                    gate_up(u + 2, l, j, 0, i + 1, i)
                    gate_up(u + 3, l, j, 1, i + 1, i)
                    down(u + 4, l, j, i, i)
                down(u + 32, l, j, STEPS - 1)

            def output_projection(u, w):
                for n in range(4):
                    col = COLS * (1 - n % 2)
                    columns(u + n, w, [col, col + COLS // 2], n // 2)

            load_x(0)
            load_gain(0)
            ffn(0, [1, 2])
            fox_units = sorted([(QK[g], [g * 2 * P, D + g * 2 * P]) for g in range(4)]
                               + [(V[g], [2 * D + g * COLS, 2 * D + g * COLS + COLS // 2]) for g in range(2)])
            for u, cols in fox_units:
                for half in range(2):
                    columns(U_FOX + u + half, a_w_in[0], cols, half)
                if u == V[0]:
                    load_gain(3)
                    load_gain(4)
            output_projection(U_FOX + F_OUT, a_w_o[0])
            ffn(1, [5, 6, 7])
            for half in range(2):
                columns(U_KV + half, b_w_kv, [0, COLS // 2], half)
            ffn(2, [8, 9])
            for n in range(4):
                columns(U_SWA + n, b_w_q[0], [(n // 2) * COLS, (n // 2) * COLS + COLS // 2], n % 2)
            load_gain(10)
            load_gain(11)
            output_projection(U_SWA + S_OUT, b_w_o[0])
            ffn(3, [12])
            for t in range(NB):
                for half in range(2):
                    cols = slice(half * COLS, (half + 1) * COLS)
                    sp.wait_ge(x_ready, QS * (SUBLAYERS - 1) + 2 * t + half + 1)
                    sp.dma_start(out[0, t * P:(t + 1) * P, cols], x[:, t, cols]).then_inc(out_done, 16)
            sp.wait_ge(out_done, 16 * QS)

        @block.gpsimd
        def _(pool):
            steps = [0]

            def chained(ins):
                steps[0] += 1
                ins.then_inc(pool_step, 1)
                pool.wait_ge(pool_step, steps[0])

            def reciprocal_rms(sums_of, dst, ready, n):
                t = n % NB
                chained(sums_of(r_tmp[:, n % 2, t:t + 1]))
                nc.gpsimd.tensor_tensor(dst[:, t:t + 1], r_tmp[:, n % 2, t:t + 1], half_power[:, :],
                                        ALU.pow).then_inc(ready, 1)

            def rms_y(b, t):
                pool.wait_ge(sq_y_ready, QS * b + 2 * t + 2)
                reciprocal_rms(lambda dst: nc.gpsimd.tensor_scalar(dst, ss_y[:, t, 0:1], ss_y[:, t, 1:2],
                                                                   WEIGHT[b] * EPS, ALU.add, ALU.add),
                               r_y, r_y_ready, NB * b + t)

            def rms_x(version, t):
                pool.wait_ge(sq_x_ready, NB * version + t + 1)
                reciprocal_rms(lambda dst: nc.gpsimd.tensor_scalar(dst, ss_x[:, t:t + 1], 1.0 / D, EPS, ALU.mult,
                                                                   ALU.add),
                               r_x, r_x_ready, NB * version + t)

            chained(nc.gpsimd.memset(half_power[:, :], -0.5))
            nc.gpsimd.memset(zeros[:, :].bitcast(F32), 0.0).then_inc(zeros_ready, 1)
            nc.gpsimd.memset(wf_hi[:, :, :].bitcast(F32), 0.0).then_inc(zeros_ready, 1)
            nc.gpsimd.memset(wf_lo[:, :, :].bitcast(F32), 0.0).then_inc(zeros_ready, 1)
            for v in range(SUBLAYERS + 1):
                for t in range(NB if v else 0):
                    rms_y(v - 1, t)
                for t in range(NB if v < SUBLAYERS else 0):
                    rms_x(v, t)

        @block.scalar
        def _(act):
            act.dma_start(table[:, 0:P], tables[:, 0:P]).then_inc(ident_landed, 16)

            tables_loaded = [0]

            def load_table(func):
                n = tables_loaded[0]
                tables_loaded[0] += 1
                nc.scalar.activation(unread[:, n:n + 1], half_power[:, :], func)

            def split(u, i=0):
                act.wait_ge(raw_landed[u % RING], DMAS * 16 * (u // RING + 1) + DMAS * 16 * i)
                if u >= RING or looped(i):
                    act.wait_ge(unit_used, u - RING + 1 + 3 * i)
                nc.scalar.activation(w_hi[:, u % RING], w_raw[:, u % RING], ACT.Copy).then_inc(hi_ready, 1)

            def split_in_halves(u):
                act.wait_ge(raw_landed[u], DMAS * 16)
                nc.scalar.activation(w_hi[:, u, 0:2], w_raw[:, u, 0:2], ACT.Copy).then_inc(hi_half_ready, 1)
                nc.scalar.activation(w_hi[:, u, 2:4], w_raw[:, u, 2:4], ACT.Copy).then_inc(hi_ready, 1)

            squared = []

            def square(src, dst, ready, value, scale=1.0):
                if squared:
                    act.wait_ge(*squared[-1])
                squared.append((ready, value))
                nc.scalar.activation(squares[:, 0:src.shape[-1]], src, ACT.Square, scale=scale,
                                     accum_out=dst).then_inc(ready, 1)

            def square_y(b, t, half):
                square(ps[:, Y + 2 * t + half, :], ss_y[:, t, half:half + 1], sq_y_ready,
                       QS * b + 2 * t + half + 1, scale=float(np.sqrt(WEIGHT[b] / D)))

            def square_x(version):
                for t in range(NB):
                    if version == 0:
                        act.wait_ge(x_landed[t], 16)
                    else:
                        act.wait_ge(x_ready, QS * (version - 1) + 2 * t + 2)
                    square(x[:, t, :], ss_x[:, t:t + 1], sq_x_ready, NB * version + t + 1)

            def xt_part(k, t, half):
                n = 2 * t + half
                act.wait_ge(xt_raw, QS * k + n + 1)
                nc.scalar.activation(xt_hi[:, k % 2, 4 * half:4 * half + 4, t * P:(t + 1) * P],
                                     ps[:, n, :].rearrange("p (c t) -> p c t", t=P),
                                     ACT.Copy).then_inc(xt_hi_ready, 1)

            def boundary(b, last_unit, k):
                act.wait_ge(y0_ready, b + 1)
                square_y(b, 0, 0)
                square_y(b, 0, 1)
                if k is not None:
                    split(last_unit + 2)
                    xt_part(k, 0, 0)
                act.wait_ge(unit_used, last_unit + 1)
                square_y(b, 1, 0)
                if k is not None:
                    xt_part(k, 0, 1)
                square_y(b, 1, 1)
                if k is not None:
                    split(last_unit + 3)
                    xt_part(k, 1, 0)
                    xt_part(k, 1, 1)
                    square_x(VERSION[k])

            def silu_step(f, u, n, i=0, first=False):
                for t in range(NB):
                    if t == 0:
                        act.wait_ge(gu0_ready, n + 1 + i)
                    else:
                        act.wait_ge(unit_used, u + 1 + 3 * i)
                    if first:
                        act.wait_ge(r_x_ready, NB * VERSION[FFN_PREP[f]] + t + 1)
                    if n > 0 or looped(i):
                        act.wait_ge(hid_ready, NB * (n + i) - NB + t + 1)
                    nc.scalar.activation(silu[:, t, :], ps[:, GU[t], 0:FC], ACT.Silu,
                                         scale=r_x[:, t:t + 1]).then_inc(silu_ready, 1)

            def ht_part(n, i=0, dst=ht_hi):
                act.wait_ge(ht_raw, n + 1 + i)
                nc.scalar.activation(dst[:, :, :], ps[:, HT, :].rearrange("p (c t) -> p c t", c=2),
                                     ACT.Copy).then_inc(ht_hi_ready, 1)

            def ffn(f):
                u, n = U_FFN[f], STEPS * f
                silu_step(f, u + 1, n, first=True)
                split(u + 3)
                ht_part(n)
                split(u + 4)
                with act.Fori(1, STEPS - 1) as i:
                    split(u + 2, i)
                    silu_step(f, u, n, i)
                    split(u + 3, i)
                    ht_part(n, i)
                    split(u + 4, i)
                split(u + 32)
                silu_step(f, u + 30, n + STEPS - 1)
                if f < 3:
                    split(u + 33)
                ht_part(n + STEPS - 1, dst=ht_last_hi)

            def rows_out(last_unit, dst, bank=ROWS[0]):
                act.wait_ge(unit_used, last_unit + 1)
                act.wait_ge(r_x_ready, NB * VERSION[P_FOX if last_unit < U_FFN1 else P_SWA] + NB)
                nc.scalar.activation(dst, ps[:, bank, :], ACT.Copy, scale=r_x[:, 0:1]).then_inc(rows_act, 1)

            def heads_out(name, dst, scale):
                act.wait_ge(rows_t, made(TURN_ORDER, name))
                nc.scalar.activation(dst, ps[:, turn_banks(name)[0], :].rearrange("p (c t) -> p c t", c=2), ACT.Copy,
                                     scale=scale).then_inc(heads_act, 1)

            def exps(pair):
                b, s, windowed = pair % 2, pair % 3, pair >= PAIRS
                act.wait_ge(neg_mx_ready, pair + 1)
                for j in range(2):
                    for t, cols in enumerate((slice(0, P), slice(P, SEG))):
                        last = nc.scalar.activation(probs[:, s, j, cols], probs[:, s, j, cols], ACT.Exp,
                                                    bias=neg_mx[:, b, j, t:t + 1], accum_out=sums[:, b, j, t:t + 1])
                if windowed:
                    last = nc.scalar.activation(sink_e[:, b], sink_d[:, b], ACT.Exp)
                last.then_inc(exp_ready, 1)

            def probs_t_out(pair):
                act.wait_ge(pt_raw, pair + 1)
                if pair >= 2:
                    act.wait_ge(ot_raw, pair - 1)
                for j in range(2):
                    last = nc.scalar.activation(probs_t[:, pair % 2, j, :], ps[:, PTB[j], 0:SEG], ACT.Copy)
                last.then_inc(pt_ready, 1)

            def ot_part(pair):
                act.wait_ge(ot_raw, pair + 1)
                nc.scalar.activation(xt_hi[:, 0, pair % PAIRS, :], ps[:, ot_bank(pair), 0:NB * P], ACT.Copy)\
                  .then_inc(ot_hi_ready, 1)

            def qk_rows_out(g):
                rows_out(U_FOX + QK[g] + 1, rows[:, 0, :], bank=(ROWS if g else FIRST_ROWS)[0])

            def q_out(g):
                heads_out(f"qk{g}", q_t[:, 2 * g:2 * g + 2, :], DH ** -0.5)

            act.wait_ge(pool_step, 1)
            load_table(ACT.Silu)
            xt_part(0, 0, 0)
            xt_part(0, 0, 1)
            split_in_halves(0)
            xt_part(0, 1, 0)
            xt_part(0, 1, 1)
            split_in_halves(1)
            square_x(0)
            split(2)
            act.dma_start(table[:, P:], tables[:, P:]).then_inc(table_landed, 16)
            act.dma_start(wf_raw[:, :, :], a_w_in[0, :, 3 * D:3 * D + H].rearrange("(k p) h -> p k h", p=P))\
               .then_inc(small_landed, 16)
            act.dma_start(bf[:, :], a_b_f[0].partition_broadcast(P)).then_inc(small_landed, 16)
            act.dma_start(sinks[:, :], b_sinks[0].partition_broadcast(P)).then_inc(small_landed, 16)
            ffn(0)

            U = U_FOX
            act.wait_ge(small_landed, 48)
            act.wait_ge(zeros_ready, 3)
            nc.scalar.activation(pick[:, :], ident[0:H, 0:H], ACT.Copy)
            nc.scalar.activation(wf_hi[:, :, 0:H], wf_raw[:, :, :], ACT.Copy).then_inc(wf_hi_ready, 1)
            boundary(0, U - 1, P_FOX)
            qk_rows_out(0)
            split(U + 3)
            act.wait_ge(f_raw, 1)
            nc.scalar.activation(f_rows[:, :], ps[0:H, 0, 0:NB * P], ACT.Copy).then_inc(f_rows_ready, 1)
            q_out(0)
            split(U + 4)
            act.wait_ge(fz_ready, 1)
            nc.scalar.activation(fz[:, 2], fz[:, 1], ACT.Exp).then_inc(act_step, 1)
            act.wait_ge(act_step, 1)
            nc.scalar.activation(fz[:, 3], fz[:, 2], ACT.Ln, bias=1.0).then_inc(fe_ready, 1)
            split(U + 5)
            act.wait_ge(c_raw, 1)
            nc.scalar.activation(c_hi[:, :], ps[0:H, 1, 0:NB * P], ACT.Copy)
            nc.scalar.activation(c_tok[:, :, :], ps[:, 1, NB * P:NB * P + NB * H].rearrange("p (t h) -> p t h", h=H),
                                 ACT.Copy).then_inc(c_ready, 1)
            load_table(ACT.Exp)
            rows_out(U + V[0] + 1, v_rows[:, 0, 0:COLS], bank=V0_BANKS[0])
            split(U + 6)
            exps(0)
            probs_t_out(0)
            split(U + 7)
            exps(1)
            qk_rows_out(1)
            ot_part(0)
            q_out(1)
            probs_t_out(1)
            split(U + 8)
            exps(2)
            ot_part(1)
            probs_t_out(2)
            split(U + 9)
            exps(3)
            qk_rows_out(2)
            ot_part(2)
            q_out(2)
            probs_t_out(3)
            split(U + 10)
            exps(4)
            ot_part(3)
            probs_t_out(4)
            split(U + 11)
            rows_out(U + V[1] + 1, v_rows[:, 0, COLS:D])
            split(U + 12)
            exps(5)
            ot_part(4)
            probs_t_out(5)
            split(U + 13)
            qk_rows_out(3)
            ot_part(5)
            q_out(3)
            split(U + 14)
            exps(6)
            exps(7)
            probs_t_out(6)
            split(U + 15)
            ot_part(6)
            probs_t_out(7)
            split(U + 16)
            ot_part(7)
            load_table(ACT.Silu)
            boundary(1, U_FFN1 - 1, 2)
            ffn(1)

            boundary(2, U_KV - 1, P_KV)
            xt_part(4, 0, 0)
            xt_part(4, 0, 1)
            split(U_FFN2 + 1)
            act.wait_ge(unit_used, U_KV + 2)
            act.wait_ge(r_x_ready, NB * VERSION[P_KV] + NB)
            for twin in range(2):
                nc.scalar.activation(rows[:, 0, :].rearrange("p (h s d) -> p h s d", s=2, d=DH)[:, :, twin, :],
                                     ps[:, FIRST_ROWS[0], 0:KVH * DH].rearrange("p (h d) -> p h d", d=DH), ACT.Copy,
                                     scale=r_x[:, 0:1])
            nc.scalar.activation(v_rows[:, 0, 0:KVH * DH], ps[:, FIRST_ROWS[0], KVH * DH:COLS], ACT.Copy,
                                 scale=r_x[:, 0:1]).then_inc(rows_act, 1)
            xt_part(4, 1, 0)
            xt_part(4, 1, 1)
            split(U_FFN2 + 2)
            heads_out("kv", k_t[:, 0:2, :], 1.0)
            ffn(2)

            U = U_SWA
            boundary(3, U - 1, P_SWA)
            split(U + 3)
            rows_out(U + 1, rows[:, 0, :], bank=FIRST_ROWS[0])
            heads_out("q0", q_t[:, 0:2, :], DH ** -0.5)
            load_table(ACT.Exp)
            split(U + 4)
            exps(PAIRS)
            split(U + 5)
            exps(PAIRS + 1)
            for pair in range(PAIRS, 2 * PAIRS):
                probs_t_out(pair)
                if pair == PAIRS + 1:
                    heads_out("q1", q_t[:, 4:6, :], DH ** -0.5)
                if pair == PAIRS + 5:
                    ot_part(pair)
                if pair + 2 < 2 * PAIRS:
                    exps(pair + 2)
                if pair == PAIRS:
                    rows_out(U + 3, rows[:, 0, :], bank=Q1_BANKS[0])
                elif pair >= 2 * PAIRS - 2:
                    split(U + 7 + pair % 2)
                if pair != PAIRS + 5:
                    ot_part(pair)
                if pair == PAIRS + 3:
                    split(U + 6)
            load_table(ACT.Silu)
            boundary(4, U_FFN3 - 1, 6)
            ffn(3)
            boundary(5, U_FFN3 + N_FFN - 1, None)

        @block.vector
        def _(dve):
            steps = [0]

            def chained(ins):
                steps[0] += 1
                ins.then_inc(dve_step, 1)
                dve.wait_ge(dve_step, steps[0])

            def split(u, i=0):
                dve.wait_ge(hi_ready, u + 1 + 3 * i)
                nc.vector.tensor_tensor(w_lo[:, u % RING], w_raw[:, u % RING], w_hi[:, u % RING].bitcast(F32),
                                        ALU.subtract).then_inc(lo_ready, 1)

            def split_half(u, n):
                part = (slice(None), u % RING, slice(2 * n, 2 * n + 2))
                if n == 0 and u < 2:
                    dve.wait_ge(hi_half_ready, u + 1)
                else:
                    dve.wait_ge(hi_ready, u + 1)
                nc.vector.tensor_tensor(w_lo[part], w_raw[part], w_hi[part].bitcast(F32),
                                        ALU.subtract).then_inc(lo_ready if n else lo_half_ready, 1)

            def gain(m, half):
                dve.wait_ge(gain_landed[m % GAINS], 16 * (m // GAINS + 1))
                return gains[:, m % GAINS, half * COLS:(half + 1) * COLS]

            def pregain(k, t, half):
                cols = slice(half * COLS, (half + 1) * COLS)
                nc.vector.tensor_tensor(xg[:, t, cols], x[:, t, cols], gain(PRE[k], half), ALU.mult)\
                  .then_inc(xg_ready, 1)

            def output_times_gain(b, t, half):
                dve.wait_ge(sq_y_ready, QS * b + 2 * t + half + 1)
                steps[0] += 1
                nc.vector.tensor_tensor(xg[:, t, half * COLS:(half + 1) * COLS], ps[:, Y + 2 * t + half, :],
                                        gain(POST[b], half), ALU.mult).then_inc(dve_step, 1)
                return steps[0]

            def residual(b, t, half, step):
                cols = slice(half * COLS, (half + 1) * COLS)
                dve.wait_ge(r_y_ready, NB * b + t + 1)
                dve.wait_ge(dve_step, step)
                nc.vector.scalar_tensor_tensor(out=x[:, t, cols], in0=xg[:, t, cols], scalar=r_y[:, t:t + 1],
                                               in1=x[:, t, cols], op0=ALU.mult, op1=ALU.add).then_inc(x_ready, 1)

            def next_gain(b, k, t, half):
                dve.wait_ge(x_ready, QS * b + 2 * t + half + 1)
                pregain(k, t, half)

            def xt_part(k, t, half):
                n = 2 * t + half
                dve.wait_ge(xt_hi_ready, QS * k + n + 1)
                cols = (slice(None), k % 2, slice(4 * half, 4 * half + 4), slice(t * P, (t + 1) * P))
                nc.vector.tensor_tensor(xt_lo[cols], ps[:, n, :].rearrange("p (c t) -> p c t", t=P),
                                        xt_hi[cols].bitcast(F32), ALU.subtract).then_inc(xt_ready, 1)

            def boundary(b, last_unit, k):
                scaled = [output_times_gain(b, 0, half) for half in range(2)]
                for half in range(2):
                    residual(b, 0, half, scaled[half])
                    next_gain(b, k, 0, half)
                xt_part(k, 0, 0)
                scaled = [output_times_gain(b, 1, 0)]
                xt_part(k, 0, 1)
                split_half(last_unit + 2, 0)
                residual(b, 1, 0, scaled[0])
                next_gain(b, k, 1, 0)
                split_half(last_unit + 2, 1)
                xt_part(k, 1, 0)
                scaled.append(output_times_gain(b, 1, 1))
                residual(b, 1, 1, scaled[1])
                next_gain(b, k, 1, 1)
                xt_part(k, 1, 1)

            def hid_step(n, i=0):
                for t in range(NB):
                    dve.wait_ge(silu_ready, NB * n + t + 1 + NB * i)
                    if n > 0 or looped(i):
                        dve.wait_ge(ht_raw, n + i)
                    nc.vector.scalar_tensor_tensor(out=hid[:, t, :], in0=ps[:, GU[t], FC:2 * FC],
                                                   scalar=r_x[:, t:t + 1], in1=silu[:, t, :], op0=ALU.mult,
                                                   op1=ALU.mult).then_inc(hid_ready, 1)

            def ht_part(n, i=0, hi=ht_hi, lo=ht_lo):
                dve.wait_ge(ht_hi_ready, n + 1 + i)
                nc.vector.tensor_tensor(lo[:, :, :], ps[:, HT, :].rearrange("p (c t) -> p c t", c=2),
                                        hi[:, :, :].bitcast(F32), ALU.subtract).then_inc(ht_ready, 1)

            def ffn(f):
                u, n = U_FFN[f], STEPS * f
                hid_step(n)
                split(u + 3)
                ht_part(n)
                split(u + 4)
                with dve.Fori(1, STEPS - 1) as i:
                    split(u + 2, i)
                    hid_step(n, i)
                    split(u + 3, i)
                    ht_part(n, i)
                    split(u + 4, i)
                split(u + 32)
                hid_step(n + STEPS - 1)
                ht_part(n + STEPS - 1, hi=ht_last_hi, lo=ht_last_lo)
                if f < 3:
                    split(u + 33)

            def rows_out(last_unit, dst, bank=ROWS[1]):
                dve.wait_ge(unit_used, last_unit + 1)
                dve.wait_ge(r_x_ready, NB * VERSION[P_FOX if last_unit < U_FFN1 else P_SWA] + NB)
                nc.vector.tensor_scalar(dst, ps[:, bank, :], r_x[:, 1:2], None, ALU.mult).then_inc(rows_dve, 1)

            def heads_out(name, dst, scale):
                dve.wait_ge(rows_t, made(TURN_ORDER, name))
                nc.vector.tensor_scalar(dst, ps[:, turn_banks(name)[1], :].rearrange("p (c t) -> p c t", c=2), scale, None,
                                        ALU.mult).then_inc(heads_dve, 1)

            def logits(pair):
                p, b, s, windowed = pair % PAIRS, pair % 2, pair % 3, pair >= PAIRS
                if not windowed:
                    dve.wait_ge(cb_raw, p + 1)
                    spread = ps[:, CB, :].rearrange("p (h s) -> p h s", h=2)
                    for cols, src in ((slice(0, P), slice(0, P)), (slice(P, SEG), slice(0, 2 * P))):
                        width = cols.stop - cols.start
                        last = nc.vector.scalar_tensor_tensor(
                            out=decay[:, :, cols], in0=spread[:, :, src], scalar=-1.0,
                            in1=causal[:, cols].unsqueeze(1).to_broadcast([P, 2, width]), op0=ALU.mult, op1=ALU.add)
                    last.then_inc(decay_ready, 1)
                    dve.wait_ge(decay_ready, p + 1)
                dve.wait_ge(sc_raw, pair + 1)
                if pair >= 3:
                    dve.wait_ge(pt_raw, pair - 2)
                for j in range(2):
                    h = 2 * p + j
                    if windowed:
                        slope = float(np.float32(2.0) ** np.float32(-8.0 * (h + 1) / H))
                        last = nc.vector.scalar_tensor_tensor(out=probs[:, s, j, :], in0=dist, scalar=-slope,
                                                              in1=ps[:, SC[j], 0:SEG], op0=ALU.mult, op1=ALU.add)
                    else:
                        for t, cols in enumerate((slice(0, P), slice(P, SEG))):
                            last = nc.vector.scalar_tensor_tensor(
                                out=probs[:, s, j, cols], in0=ps[:, SC[j], cols], scalar=c_tok[:, t, h:h + 1],
                                in1=decay[:, j, cols], op0=ALU.add, op1=ALU.add)
                last.then_inc(logits_done, 1)
                dve.wait_ge(logits_done, pair + 1)
                nc.vector.reduce_max(mx[:, b, :, 0], probs[:, s, :, 0:P], AX.X)
                chained(nc.vector.reduce_max(mx[:, b, :, 1], probs[:, s, :, P:SEG], AX.X))
                if windowed:
                    sink = sinks[:, 2 * p:2 * p + 2].unsqueeze(2).to_broadcast([P, 2, NB])
                    chained(nc.vector.tensor_tensor(mx[:, b], mx[:, b], sink, ALU.max))
                    nc.vector.tensor_tensor(sink_d[:, b], sink, mx[:, b], ALU.subtract)
                nc.vector.tensor_scalar(neg_mx[:, b], mx[:, b], -1.0, None, ALU.mult).then_inc(neg_mx_ready, 1)

            def normalise(pair):
                b, s = pair % 2, pair % 3
                dve.wait_ge(exp_ready, pair + 1)
                if pair >= PAIRS:
                    chained(nc.vector.tensor_tensor(sums[:, b], sums[:, b], sink_e[:, b], ALU.add))
                chained(nc.vector.reciprocal(recip[:, b], sums[:, b]))
                for j in range(2):
                    for t, cols in enumerate((slice(0, P), slice(P, SEG))):
                        last = nc.vector.tensor_scalar(probs[:, s, j, cols], probs[:, s, j, cols],
                                                       recip[:, b, j, t:t + 1], None, ALU.mult)
                last.then_inc(probs_ready, 1)

            def ot_part(pair):
                dve.wait_ge(ot_hi_ready, pair + 1)
                nc.vector.tensor_tensor(xt_lo[:, 0, pair % PAIRS, :], ps[:, ot_bank(pair), 0:NB * P],
                                        xt_hi[:, 0, pair % PAIRS, :].bitcast(F32), ALU.subtract).then_inc(ot_ready, 1)

            def qk_rows_out(g):
                rows_out(U_FOX + QK[g] + 1, rows[:, 1, :], bank=(ROWS if g else FIRST_ROWS)[1])

            def k_out(g):
                heads_out(f"qk{g}", k_t[:, 2 * g:2 * g + 2, :], 1.0)

            for t in range(NB):
                dve.wait_ge(x_landed[t], 16)
                for half in range(2):
                    pregain(0, t, half)
                if t == 0:
                    for half in range(2):
                        xt_part(0, 0, half)
            split_half(0, 0)
            split_half(0, 1)
            for half in range(2):
                xt_part(0, 1, half)
            split_half(1, 0)
            split_half(1, 1)
            split(2)
            ffn(0)

            U = U_FOX
            dve.wait_ge(wf_hi_ready, 1)
            dve.wait_ge(table_landed, 16)
            nc.vector.tensor_tensor(wf_lo[:, :, 0:H], wf_raw[:, :, :], wf_hi[:, :, 0:H].bitcast(F32),
                                    ALU.subtract).then_inc(wf_ready, 1)
            boundary(0, U - 1, P_FOX)
            split(U + 2)
            qk_rows_out(0)
            split(U + 3)
            k_out(0)
            dve.wait_ge(f_t_raw, 1)
            f_tok = ps[:, 1, 0:NB * H].rearrange("p (t h) -> p t h", h=H)
            for t in range(NB):
                last = nc.vector.scalar_tensor_tensor(out=fz[:, 0, t, :], in0=f_tok[:, t, :], scalar=r_x[:, t:t + 1],
                                                      in1=bf[:, :], op0=ALU.mult, op1=ALU.add)
            chained(last)
            chained(nc.vector.scalar_tensor_tensor(out=fz[:, 1], in0=fz[:, 0], scalar=-1.0, in1=fz[:, 0],
                                                   op0=ALU.mult, op1=ALU.min))
            nc.vector.tensor_scalar(fz[:, 0], fz[:, 0], 0.0, None, ALU.min).then_inc(fz_ready, 1)
            split(U + 4)
            dve.wait_ge(fe_ready, 1)
            nc.vector.tensor_tensor(logf[:, :, :], fz[:, 0], fz[:, 3], ALU.subtract).then_inc(logf_ready, 1)
            split(U + 5)
            dve.wait_ge(c_ready, 1)
            nc.vector.tensor_tensor(c_lo[:, :], ps[0:H, 1, 0:NB * P], c_hi[:, :].bitcast(F32),
                                    ALU.subtract).then_inc(c_lo_ready, 1)
            rows_out(U + V[0] + 1, v_rows[:, 1, 0:COLS], bank=V0_BANKS[1])
            logits(0)
            split(U + 6)
            normalise(0)
            logits(1)
            split(U + 7)
            qk_rows_out(1)
            normalise(1)
            ot_part(0)
            k_out(1)
            logits(2)
            split(U + 8)
            normalise(2)
            ot_part(1)
            logits(3)
            split(U + 9)
            qk_rows_out(2)
            normalise(3)
            ot_part(2)
            k_out(2)
            logits(4)
            split(U + 10)
            normalise(4)
            ot_part(3)
            split(U + 11)
            rows_out(U + V[1] + 1, v_rows[:, 1, COLS:D])
            logits(5)
            split(U + 12)
            normalise(5)
            ot_part(4)
            split(U + 13)
            qk_rows_out(3)
            ot_part(5)
            k_out(3)
            logits(6)
            logits(7)
            normalise(6)
            split(U + 14)
            normalise(7)
            ot_part(6)
            split(U + 15)
            ot_part(7)
            split(U + 16)
            boundary(1, U_FFN1 - 1, 2)
            split(U_FFN1 + 2)
            ffn(1)

            boundary(2, U_KV - 1, P_KV)
            for half in range(2):
                dve.wait_ge(xt_raw, QS * P_KV + 2)
                pregain(4, 0, half)
            split(U_FFN2)
            xt_part(4, 0, 0)
            xt_part(4, 0, 1)
            split(U_FFN2 + 1)
            for half in range(2):
                dve.wait_ge(xt_raw, QS * P_KV + 4)
                pregain(4, 1, half)
            dve.wait_ge(unit_used, U_KV + 2)
            dve.wait_ge(r_x_ready, NB * VERSION[P_KV] + NB)
            for twin in range(2):
                nc.vector.tensor_scalar(rows[:, 1, :].rearrange("p (h s d) -> p h s d", s=2, d=DH)[:, :, twin, :],
                                        ps[:, FIRST_ROWS[1], 0:KVH * DH].rearrange("p (h d) -> p h d", d=DH), r_x[:, 1:2],
                                        None, ALU.mult)
            nc.vector.tensor_scalar(v_rows[:, 1, 0:KVH * DH], ps[:, FIRST_ROWS[1], KVH * DH:COLS], r_x[:, 1:2], None,
                                    ALU.mult).then_inc(rows_dve, 1)
            xt_part(4, 1, 0)
            xt_part(4, 1, 1)
            split(U_FFN2 + 2)
            heads_out("kv", k_t[:, 2:4, :], 1.0)
            ffn(2)

            U = U_SWA
            boundary(3, U - 1, P_SWA)
            split(U + 2)
            rows_out(U + 1, rows[:, 1, :], bank=FIRST_ROWS[1])
            split(U + 3)
            heads_out("q0", q_t[:, 2:4, :], DH ** -0.5)
            logits(PAIRS)
            logits(PAIRS + 1)
            normalise(PAIRS)
            logits(PAIRS + 2)
            for pair in range(PAIRS, 2 * PAIRS):
                if pair == PAIRS + 1:
                    rows_out(U + 3, rows[:, 1, :], bank=Q1_BANKS[1])
                if pair in (PAIRS + 2, PAIRS + 6):
                    ot_part(pair - 1)
                if pair + 1 < 2 * PAIRS:
                    normalise(pair + 1)
                if pair > PAIRS and pair not in (PAIRS + 2, PAIRS + 6):
                    ot_part(pair - 1)
                if PAIRS < pair < 2 * PAIRS - 2:
                    logits(pair + 2)
                if pair == PAIRS + 1:
                    heads_out("q1", q_t[:, 6:8, :], DH ** -0.5)
                    split(U + 4)
                elif pair == PAIRS + 2:
                    split(U + 5)
                elif pair == PAIRS + 4:
                    split(U + 6)
            split(U + 7)
            split(U + 8)
            ot_part(2 * PAIRS - 1)
            boundary(4, U_FFN3 - 1, 6)
            split(U_FFN3 + 2)
            ffn(3)
            for t in range(NB):
                scaled = [output_times_gain(5, t, half) for half in range(2)]
                for half in range(2):
                    residual(5, t, half, scaled[half])

        @block.tensor
        def _(pe):
            def transpose_x(k, t, half):
                pe.wait_ge(xg_ready, QS * k + 2 * t + half + 1)
                for c in range(4):
                    last = nc.tensor.transpose(ps[:, 2 * t + half, c * P:(c + 1) * P],
                                               xg[:, t, (4 * half + c) * P:(4 * half + c + 1) * P], ident)
                last.then_inc(xt_raw, 1)

            def half_unit(u, t, parity, half, bank, chunks=range(4)):
                slot = u % RING
                for k in chunks:
                    left = (slice(None), parity, 4 * half + k, slice(t * P, (t + 1) * P))
                    start, stop = half == 0 and k == 0, half == 1 and k == 3
                    nc.tensor.matmul(ps[:, bank, :], xt_hi[left], w_hi[:, slot, k, :], start=start, stop=False)
                    nc.tensor.matmul(ps[:, bank, :], xt_hi[left], w_lo[:, slot, k, :], start=False, stop=False)
                    last = nc.tensor.matmul(ps[:, bank, :], xt_lo[left], w_hi[:, slot, k, :], start=False, stop=stop)
                return last

            def unit(u, parity, half, banks, block0_done=None, i=0):
                pe.wait_ge(lo_ready, u + 1 + 3 * i)
                last = half_unit(u, 0, parity, half, banks[0])
                if block0_done is not None:
                    last.then_inc(block0_done, 1)
                half_unit(u, 1, parity, half, banks[1]).then_inc(unit_used, 1)

            def block0_of_first_units(k, u, parity, bank):
                for half in range(2):
                    transpose_x(k, 0, half)
                pe.wait_ge(xt_ready, QS * k + 1)
                pe.wait_ge(lo_ready, u + 1)
                half_unit(u, 0, parity, 0, bank)
                pe.wait_ge(xt_ready, QS * k + 2)
                pe.wait_ge(lo_half_ready, 2 + BOUNDARY[k] + 1)
                half_unit(u + 1, 0, parity, 1, bank, range(2))
                transpose_x(k, 1, 0)
                pe.wait_ge(lo_ready, u + 2)
                return half_unit(u + 1, 0, parity, 1, bank, range(2, 4))

            def block1_of_first_unit(k, u, parity, bank):
                pe.wait_ge(xt_ready, QS * k + 3)
                half_unit(u, 1, parity, 0, bank, range(2))
                if k > 0:
                    transpose_x(k, 1, 1)
                half_unit(u, 1, parity, 0, bank, range(2, 4)).then_inc(unit_used, 1)

            def first_units(k, u, parity, banks, block0_done=None):
                if k > 0:
                    last = block0_of_first_units(k, u, parity, banks[0])
                else:
                    for t in range(NB):
                        for half in range(2):
                            transpose_x(k, t, half)
                    pe.wait_ge(xt_ready, 2)
                    for half in range(2):
                        pe.wait_ge(lo_half_ready, half + 1)
                        half_unit(u + half, 0, parity, half, banks[0], range(2))
                        pe.wait_ge(lo_ready, u + half + 1)
                        last = half_unit(u + half, 0, parity, half, banks[0], range(2, 4))
                if block0_done is not None:
                    last.then_inc(block0_done, 1)
                block1_of_first_unit(k, u, parity, banks[1])
                pe.wait_ge(xt_ready, QS * k + 4)
                half_unit(u + 1, 1, parity, 1, banks[1]).then_inc(unit_used, 1)

            def keys_values_and_first_units(u):
                k = P_KV
                block0_of_first_units(k, U_KV, 1, FIRST_ROWS[0])
                block1_of_first_unit(k, U_KV, 1, FIRST_ROWS[1])
                pe.wait_ge(xt_ready, QS * k + 4)
                half_unit(U_KV + 1, 1, 1, 1, FIRST_ROWS[1], range(2))
                transpose_x(k + 1, 0, 0)
                transpose_x(k + 1, 0, 1)
                half_unit(U_KV + 1, 1, 1, 1, FIRST_ROWS[1], range(2, 4)).then_inc(unit_used, 1)
                pe.wait_ge(xt_ready, QS * (k + 1) + 1)
                pe.wait_ge(lo_ready, u + 1)
                half_unit(u, 0, 0, 0, GU[0])
                pe.wait_ge(xt_ready, QS * (k + 1) + 2)
                pe.wait_ge(lo_ready, u + 2)
                half_unit(u + 1, 0, 0, 1, GU[0], range(2))
                transpose_x(k + 1, 1, 0)
                transpose_x(k + 1, 1, 1)
                half_unit(u + 1, 0, 0, 1, GU[0], range(2, 4)).then_inc(gu0_ready, 1)
                pe.wait_ge(xt_ready, QS * (k + 1) + 3)
                half_unit(u, 1, 0, 0, GU[1]).then_inc(unit_used, 1)
                turn("kv")
                pe.wait_ge(xt_ready, QS * (k + 1) + 4)
                half_unit(u + 1, 1, 0, 1, GU[1]).then_inc(unit_used, 1)
                heads_done("kv")

            def clear_y():
                for bank in range(Y, Y + 4):
                    nc.tensor.matmul(ps[:, bank, :], zeros[:, 0:P], zeros[:, :], start=True, stop=False,
                                     skip_group_check=True)

            def transpose_h(n, i=0):
                for t in range(NB):
                    pe.wait_ge(hid_ready, NB * n + t + 1 + NB * i)
                    for c in range(2):
                        last = nc.tensor.transpose(ps[:, HT, (2 * c + t) * P:(2 * c + t + 1) * P],
                                                   hid[:, t, c * P:(c + 1) * P], ident)
                last.then_inc(ht_raw, 1)

            def down_part(u, t, c, hi=ht_hi, lo=ht_lo, stop=False):
                slot, tokens = u % RING, slice(t * P, (t + 1) * P)
                for left, w in ((hi, w_hi), (hi, w_lo), (lo, w_hi)):
                    for half in range(2):
                        last = nc.tensor.matmul(ps[:, Y + 2 * t + half, :], left[:, c, tokens],
                                                w[:, slot, 2 * c + half, :], start=False,
                                                stop=stop and left is lo, skip_group_check=True)
                return last

            def down(u, n, i=0):
                pe.wait_ge(ht_ready, n + 1 + i)
                pe.wait_ge(lo_ready, u + 1 + 3 * i)
                for t in range(NB):
                    for c in range(2):
                        last = down_part(u, t, c)
                last.then_inc(unit_used, 1)

            def ffn(f):
                u, n, k = U_FFN[f], STEPS * f, FFN_PREP[f]
                if k == P_KV + 1:
                    keys_values_and_first_units(u)
                else:
                    first_units(k, u, 0, GU, block0_done=gu0_ready)
                clear_y()
                with pe.Fori(0, STEPS - 2) as i:
                    transpose_h(n, i)
                    unit(u + 2, 0, 0, GU, i=i)
                    unit(u + 3, 0, 1, GU, block0_done=gu0_ready, i=i)
                    down(u + 4, n, i=i)
                n += STEPS - 2
                transpose_h(n)
                unit(u + 29, 0, 0, GU)
                unit(u + 30, 0, 1, GU, block0_done=gu0_ready)
                pe.wait_ge(ht_ready, n + 1)
                pe.wait_ge(lo_ready, u + 32)
                down_part(u + 31, 0, 0)
                down_part(u + 31, 0, 1)
                transpose_h(n + 1)
                down_part(u + 31, 1, 0)
                pe.wait_ge(ht_ready, n + 2)
                pe.wait_ge(lo_ready, u + 33)
                down_part(u + 32, 0, 0, ht_last_hi, ht_last_lo)
                down_part(u + 32, 0, 1, ht_last_hi, ht_last_lo, stop=True).then_inc(y0_ready, 1)
                down_part(u + 31, 1, 1).then_inc(unit_used, 1)
                down_part(u + 32, 1, 0, ht_last_hi, ht_last_lo)
                down_part(u + 32, 1, 1, ht_last_hi, ht_last_lo, stop=True).then_inc(unit_used, 1)

            def rows_done(name):
                pe.wait_ge(rows_act, made(ROW_ORDER, name))
                pe.wait_ge(rows_dve, made(ROW_ORDER, name))

            def heads_done(name):
                pe.wait_ge(heads_act, made(TURN_ORDER, name))
                pe.wait_ge(heads_dve, made(TURN_ORDER, name))

            def turn(name):
                rows_done(name)
                for c in range(4):
                    for t in range(NB):
                        at = ((c % 2) * 2 + t) * P
                        last = nc.tensor.transpose(ps[:, turn_banks(name)[c // 2], at:at + P], rows[:, t, c * P:(c + 1) * P],
                                                   ident)
                last.then_inc(rows_t, 1)

            def forget_gates():
                pe.wait_ge(wf_ready, 1)
                for c in range(DC):
                    for left, right in ((wf_hi, xt_hi), (wf_hi, xt_lo), (wf_lo, xt_hi)):
                        last = nc.tensor.matmul(ps[:, 0, 0:NB * P], left[:, c, :], right[:, P_FOX % 2, c, :],
                                                start=c == 0 and left is wf_hi and right is xt_hi,
                                                stop=c == DC - 1 and left is wf_lo)
                last.then_inc(f_raw, 1)

            def forget_tokens():
                pe.wait_ge(f_rows_ready, 1)
                for t in range(NB):
                    last = nc.tensor.transpose(ps[:, 1, t * H:(t + 1) * H], f_rows[:, t * P:(t + 1) * P],
                                               ident[0:H, 0:H])
                last.then_inc(f_t_raw, 1)

            def forget_sums():
                pe.wait_ge(logf_ready, 1)
                nc.tensor.matmul(ps[0:H, 1, 0:NB * P], logf[:, 0, :], tri_ones, start=True, stop=False)
                nc.tensor.matmul(ps[0:H, 1, P:NB * P], logf[:, 1, :], tri, start=False, stop=True)
                c = ps[:, 1, NB * P:NB * P + NB * H]
                nc.tensor.matmul(c[:, 0:H], tri, logf[:, 0, :], start=True, stop=True)
                nc.tensor.matmul(c[:, H:2 * H], ones, logf[:, 0, :], start=True, stop=False)
                nc.tensor.matmul(c[:, H:2 * H], tri, logf[:, 1, :], start=False, stop=True).then_inc(c_raw, 1)

            def scores(pair):
                p, windowed = pair % PAIRS, pair >= PAIRS
                if not windowed:
                    if p:
                        pe.wait_ge(decay_ready, p)
                    for j in range(2):
                        h = 2 * p + j
                        for part in (c_hi, c_lo):
                            last = nc.tensor.matmul(ps[:, CB, j * NB * P:(j + 1) * NB * P],
                                                    pick[:, h:h + 1].to_broadcast([H, P]), part[:, :],
                                                    start=part is c_hi, stop=part is c_lo)
                    last.then_inc(cb_raw, 1)
                if pair == PAIRS + 4:
                    heads_done("q1")
                if pair:
                    pe.wait_ge(logits_done, pair)
                for j in range(2):
                    heads = slice(j * DH, (j + 1) * DH)
                    keys = k_t[heads, p // 2 if windowed else p, :]
                    nc.tensor.matmul(ps[:, SC[j], 0:P], q_t[heads, p, 0:P], keys[:, 0:P], start=True, stop=True)
                    last = nc.tensor.matmul(ps[:, SC[j], P:SEG], q_t[heads, p, P:NB * P], keys, start=True, stop=True)
                last.then_inc(sc_raw, 1)

            def transpose_probs(pair):
                pe.wait_ge(probs_ready, pair + 1)
                if pair:
                    pe.wait_ge(pt_ready, pair)
                for j in range(2):
                    for n in range(3):
                        last = nc.tensor.transpose(ps[:, PTB[j], n * P:(n + 1) * P],
                                                   probs[:, pair % 3, j, n * P:(n + 1) * P], ident)
                last.then_inc(pt_raw, 1)

            def values(pair):
                p = pair % PAIRS
                pe.wait_ge(pt_ready, pair + 1)
                if pair:
                    pe.wait_ge(ot_ready, pair)
                if ot_bank(pair) != OT:
                    pe.wait_ge(logits_done, pair - p + PAIRS)
                for j in range(2):
                    h = (2 * p + j) // 4 if pair >= PAIRS else 2 * p + j
                    v = v_rows[:, :, h * DH:(h + 1) * DH]
                    o = ps[j * DH:(j + 1) * DH, ot_bank(pair), 0:NB * P]
                    pt = probs_t[:, pair % 2, j, :]
                    nc.tensor.matmul(o, v[:, 0, :], pt[:, 0:2 * P], start=True, stop=False)
                    last = nc.tensor.matmul(o[:, P:2 * P], v[:, 1, :], pt[:, 2 * P:SEG], start=False, stop=True)
                last.then_inc(ot_raw, 1)

            def out_part(u, n, t, pairs_done, chunks=range(4)):
                pe.wait_ge(lo_ready, u + n + 1)
                last = PAIRS - 2 if n == 1 and t == 0 else 4 * (n // 2) + chunks[-1] + 1
                pe.wait_ge(ot_ready, pairs_done + last)
                return half_unit(u + n, t, 0, n // 2, Y + 2 * t + 1 - n % 2, chunks)

            def output_rest(u, pairs_done, done=0):
                out_part(u, 2, 0, pairs_done, range(done, 3))
                values(pairs_done + PAIRS - 1)
                out_part(u, 3, 0, pairs_done, range(3))
                out_part(u, 2, 0, pairs_done, range(3, 4))
                out_part(u, 3, 0, pairs_done, range(3, 4)).then_inc(y0_ready, 1)
                out_part(u, 2, 1, pairs_done, range(done, 4)).then_inc(unit_used, 1)
                out_part(u, 3, 1, pairs_done).then_inc(unit_used, 1)

            pe.wait_ge(ident_landed, 16)
            pe.wait_ge(zeros_ready, 3)
            ffn(0)
            pe.wait_ge(table_landed, 16)

            U = U_FOX
            first_units(P_FOX, U + QK[0], 1, FIRST_ROWS)
            forget_gates()
            turn("qk0")
            forget_tokens()
            unit(U + V[0], 1, 0, V0_BANKS)
            forget_sums()
            unit(U + V[0] + 1, 1, 1, V0_BANKS)
            pe.wait_ge(c_ready, 1)
            pe.wait_ge(c_lo_ready, 1)
            heads_done("qk0")
            scores(0)
            unit(U + QK[1], 1, 0, ROWS)
            scores(1)
            rows_done("v0")
            transpose_probs(0)
            unit(U + QK[1] + 1, 1, 1, ROWS)
            values(0)
            turn("qk1")
            transpose_probs(1)
            heads_done("qk1")
            scores(2)
            unit(U + QK[2], 1, 0, ROWS)
            values(1)
            scores(3)
            transpose_probs(2)
            unit(U + QK[2] + 1, 1, 1, ROWS)
            values(2)
            turn("qk2")
            transpose_probs(3)
            heads_done("qk2")
            scores(4)
            unit(U + V[1], 1, 0, ROWS)
            values(3)
            transpose_probs(4)
            unit(U + V[1] + 1, 1, 1, ROWS)
            scores(5)
            rows_done("v1")
            unit(U + QK[3], 1, 0, ROWS)
            values(4)
            transpose_probs(5)
            unit(U + QK[3] + 1, 1, 1, ROWS)
            values(5)
            turn("qk3")
            out_part(U + F_OUT, 1, 0, 0)
            heads_done("qk3")
            scores(6)
            out_part(U + F_OUT, 0, 0, 0, range(2))
            scores(7)
            out_part(U + F_OUT, 0, 0, 0, range(2, 4))
            out_part(U + F_OUT, 0, 1, 0).then_inc(unit_used, 1)
            transpose_probs(6)
            pe.wait_ge(decay_ready, PAIRS)
            out_part(U + F_OUT, 1, 1, 0).then_inc(unit_used, 1)
            values(6)
            transpose_probs(7)
            output_rest(U + F_OUT, 0)
            ffn(1)

            ffn(2)

            U = U_SWA
            first_units(P_SWA, U, 1, FIRST_ROWS)
            pe.wait_ge(lo_ready, U + 3)
            half_unit(U + 2, 0, 1, 0, Q1_BANKS[0])
            turn("q0")
            pe.wait_ge(lo_ready, U + 4)
            half_unit(U + 3, 0, 1, 1, Q1_BANKS[0], range(1))
            heads_done("q0")
            scores(PAIRS)
            half_unit(U + 2, 1, 1, 0, Q1_BANKS[1]).then_inc(unit_used, 1)
            scores(PAIRS + 1)
            half_unit(U + 3, 0, 1, 1, Q1_BANKS[0], range(1, 4))
            first = U + S_OUT
            for pair in range(PAIRS, 2 * PAIRS):
                if pair + 2 < 2 * PAIRS:
                    scores(pair + 2)
                transpose_probs(pair)
                if pair == PAIRS:
                    half_unit(U + 3, 1, 1, 1, Q1_BANKS[1]).then_inc(unit_used, 1)
                elif pair == PAIRS + 1:
                    turn("q1")
                elif pair == PAIRS + 2:
                    out_part(first, 0, 0, PAIRS, range(0, 2))
                    out_part(first, 0, 1, PAIRS, range(0, 2))
                elif pair == PAIRS + 3:
                    out_part(first, 0, 0, PAIRS, range(2, 3))
                    out_part(first, 0, 1, PAIRS, range(2, 3))
                    out_part(first, 1, 1, PAIRS, range(0, 2))
                elif pair == PAIRS + 4:
                    out_part(first, 0, 0, PAIRS, range(3, 4))
                    out_part(first, 0, 1, PAIRS, range(3, 4)).then_inc(unit_used, 1)
                    out_part(first, 1, 1, PAIRS, range(2, 4))
                elif pair == PAIRS + 5:
                    out_part(first, 2, 0, PAIRS, range(0, 1))
                    out_part(first, 2, 1, PAIRS, range(0, 1))
                elif pair == PAIRS + 6:
                    out_part(first, 1, 0, PAIRS).then_inc(unit_used, 1)
                if pair < 2 * PAIRS - 1:
                    values(pair)
            output_rest(first, PAIRS, done=1)
            ffn(3)


_INS = ["x", "ffn_w_gate", "ffn_w_up", "ffn_w_down", "norm_g", "a_w_in", "a_b_f", "a_w_o", "kv_norm_g", "b_w_kv",
        "b_w_q", "b_sinks", "b_w_o"]
_OUTS = [((1, NB * P, D), "float32")]


def kernel(**inputs):
    import numpy as _np
    import concourse.bacc as _bacc
    from concourse import mybir as _mybir
    from concourse.bass_utils import run_bass_kernel_spmd as _run

    nc = _bacc.Bacc("TRN2", target_bir_lowering=False, num_devices=1)
    arrays, args = {}, []
    for name in [*_INS, "tables"]:
        a = _np.ascontiguousarray(constants() if name == "tables" else inputs[name])
        arrays[f"in_{name}_dram"] = a
        args.append(nc.dram_tensor(f"in_{name}_dram", a.shape, _mybir.dt.from_np(a.dtype), kind="ExternalInput").ap())
    for i, (shape, dtype) in enumerate(_OUTS):
        dt = _mybir.dt.from_np(_np.dtype(dtype))
        args.append(nc.dram_tensor(f"out_{i}_dram", shape, dt, kind="ExternalOutput").ap())
    trunk(nc, *args)
    r = _run(nc, [arrays], core_ids=[0])
    return r.results[0]["out_0_dram"]
```
